# Optimizing a Trainium2 kernel written in Bass

```python
import math
import jax, jax.numpy as jnp
from jax import lax
import numpy as np

D_MODEL = 1024
BATCH = 1
SEQ = 2048
DEPTH = 1

CHUNK = 64
RMS_EPS = 1e-6
GDN_HEADS = 8
GDN_DK = 128
GDN_DV = 128
GDN_CONV = 4
SWA_HEADS = 16
SWA_KV_HEADS = 2
SWA_HEAD_DIM = 64
SWA_WINDOW = 128
SWA_BAND_CHUNKS = SWA_WINDOW // CHUNK
REL_BUCKETS = 32
REL_MAX_DIST = 128

GDN_QK_W = GDN_HEADS * GDN_DK
GDN_V_W = GDN_HEADS * GDN_DV
GDN_CONV_CH = 2 * GDN_QK_W + GDN_V_W
SWA_Q_W = SWA_HEADS * SWA_HEAD_DIM
SWA_KV_W = SWA_KV_HEADS * SWA_HEAD_DIM
IN_SPLITS = (GDN_QK_W, GDN_QK_W, GDN_V_W, GDN_HEADS, GDN_HEADS, GDN_V_W,
             SWA_Q_W, SWA_KV_W, SWA_KV_W, SWA_Q_W, D_MODEL, D_MODEL)
D_IN = sum(IN_SPLITS)
SPLIT_POINTS = tuple(int(v) for v in np.cumsum(IN_SPLITS)[:-1])

kernel_name = "hybrid_gdn_swa_sink_gated_merge"

def rms_norm(x, w):
    xf = x.astype(jnp.float32)
    y = xf * lax.rsqrt(jnp.mean(xf * xf, axis=-1, keepdims=True) + RMS_EPS)
    return (y * w.astype(jnp.float32)).astype(x.dtype)

def l2_normalize(x):
    xf = x.astype(jnp.float32)
    return (xf * lax.rsqrt(jnp.sum(xf * xf, axis=-1, keepdims=True) + 1e-6)).astype(x.dtype)

def causal_depthwise_conv(x, w):
    K = w.shape[0]
    T = x.shape[1]
    xp = jnp.pad(x, ((0, 0), (K - 1, 0), (0, 0)))
    return sum(xp[:, k:k + T] * w[k] for k in range(K))

def t5_relative_bucket(rel):
    nb = REL_BUCKETS // 2
    ret = (rel > 0).astype(np.int32) * nb
    n = np.abs(rel)
    max_exact = nb // 2
    large = max_exact + (np.log(np.maximum(n, 1) / max_exact) / math.log(REL_MAX_DIST / max_exact)
                         * (nb - max_exact)).astype(np.int32)
    large = np.minimum(large, nb - 1)
    return (ret + np.where(n < max_exact, n, large)).astype(np.int32)

def banded_relative_bias(rel_table):
    S = SWA_BAND_CHUNKS * CHUNK
    q_pos = np.arange(CHUNK)[:, None]
    k_pos = np.arange(S)[None, :] - (SWA_BAND_CHUNKS - 1) * CHUNK
    buckets = t5_relative_bucket(k_pos - q_pos)
    return jnp.transpose(rel_table[buckets], (2, 0, 1))

def gated_delta_rule(q, k, v, g, beta):
    out_dtype = v.dtype
    B, T, H, dk = q.shape
    dv = v.shape[-1]
    NC = T // CHUNK
    f32 = jnp.float32
    q = q.astype(f32) * (dk ** -0.5)
    k = k.astype(f32)
    v = v.astype(f32)

    def vec_chunks(a):
        return a.reshape(B, NC, CHUNK, H, a.shape[-1]).transpose(1, 0, 3, 2, 4)

    def scal_chunks(a):
        return a.astype(f32).reshape(B, NC, CHUNK, H).transpose(1, 0, 3, 2)

    qc, kc, vc = vec_chunks(q), vec_chunks(k), vec_chunks(v)
    gc = jnp.cumsum(scal_chunks(g), axis=-1)
    bc = scal_chunks(beta)
    lower = np.tril(np.ones((CHUNK, CHUNK), dtype=bool))
    strict = np.tril(np.ones((CHUNK, CHUNK), dtype=bool), -1)
    decay = jnp.exp(jnp.where(lower, gc[..., :, None] - gc[..., None, :], -jnp.inf))

    kb = kc * bc[..., None]
    vb = vc * bc[..., None]
    n_mat = jnp.where(strict, -jnp.einsum('nbhid,nbhjd->nbhij', kb, kc) * decay, 0.0)
    t_mat = jnp.eye(CHUNK, dtype=f32) + n_mat
    p_mat = n_mat
    for _ in range(int(math.log2(CHUNK)) - 1):
        p_mat = jnp.einsum('nbhij,nbhjk->nbhik', p_mat, p_mat)
        t_mat = t_mat + jnp.einsum('nbhij,nbhjk->nbhik', t_mat, p_mat)

    u = jnp.einsum('nbhij,nbhjd->nbhid', t_mat, vb)
    w = jnp.einsum('nbhij,nbhjd->nbhid', t_mat, kb * jnp.exp(gc)[..., None])
    qk = jnp.einsum('nbhid,nbhjd->nbhij', qc, kc) * decay
    qg = qc * jnp.exp(gc)[..., None]
    g_last = gc[..., -1]
    kd = kc * jnp.exp(g_last[..., None] - gc)[..., None]

    def step(state, inp):
        u_i, w_i, qk_i, qg_i, kd_i, gl_i = inp
        v_new = u_i - jnp.einsum('bhcd,bhde->bhce', w_i, state)
        o_i = jnp.einsum('bhcd,bhde->bhce', qg_i, state) + jnp.einsum('bhij,bhje->bhie', qk_i, v_new)
        state = state * jnp.exp(gl_i)[..., None, None] + jnp.einsum('bhcd,bhce->bhde', kd_i, v_new)
        return state, o_i

    s0 = jnp.zeros((B, H, dk, dv), f32)
    _, o = lax.scan(step, s0, (u, w, qk, qg, kd, g_last))
    return o.transpose(1, 0, 3, 2, 4).reshape(B, T, H, dv).astype(out_dtype)

def band_keys(a, n_chunks):
    parts = []
    for j in range(SWA_BAND_CHUNKS - 1, -1, -1):
        parts.append(jnp.pad(a, ((0, 0), (j, 0), (0, 0), (0, 0), (0, 0)))[:, :n_chunks])
    return jnp.concatenate(parts, axis=2)

def swa_sink_attention(q, k, v, sinks, bias):
    B, T, Hq, D = q.shape
    Hkv = k.shape[2]
    G = Hq // Hkv
    NC = T // CHUNK
    S = SWA_BAND_CHUNKS * CHUNK
    qc = q.reshape(B, NC, CHUNK, Hkv, G, D)
    kb = band_keys(k.reshape(B, NC, CHUNK, Hkv, D), NC)
    vb = band_keys(v.reshape(B, NC, CHUNK, Hkv, D), NC)
    logits = jnp.einsum('bnqhgd,bnshd->bnhgqs', qc, kb).astype(jnp.float32) * (D ** -0.5)
    logits = logits + bias.astype(jnp.float32).reshape(Hkv, G, CHUNK, S)
    key_chunk = np.arange(NC)[:, None] - (SWA_BAND_CHUNKS - 1) + np.arange(S)[None, :] // CHUNK
    valid = key_chunk >= 0
    logits = jnp.where(valid[None, :, None, None, None, :], logits, -jnp.inf)
    sink = sinks.astype(jnp.float32).reshape(Hkv, G)[None, None, :, :, None, None]
    m = jnp.maximum(jnp.max(logits, axis=-1, keepdims=True), sink)
    p = jnp.exp(logits - m)
    probs = p / (jnp.sum(p, axis=-1, keepdims=True) + jnp.exp(sink - m))
    o = jnp.einsum('bnhgqs,bnshd->bnqhgd', probs.astype(v.dtype), vb)
    return o.reshape(B, T, Hq, D)

def hybrid_layer(x, norm_w, w_in, conv_w, a_log, dt_bias, gdn_norm_w, attn_sinks,
                 w_o_a, w_o_b, w_out, pos_bias):
    B, T, _ = x.shape
    h = rms_norm(x, norm_w)
    z = h @ w_in
    (qa, ka, va, b_a, a_a, za, qb, kb, vb, zb, gate_a, gate_b) = jnp.split(z, SPLIT_POINTS, axis=-1)

    qkv = jax.nn.silu(causal_depthwise_conv(jnp.concatenate([qa, ka, va], axis=-1), conv_w))
    qa, ka, va = jnp.split(qkv, (GDN_QK_W, 2 * GDN_QK_W), axis=-1)
    qa = l2_normalize(qa.reshape(B, T, GDN_HEADS, GDN_DK))
    ka = l2_normalize(ka.reshape(B, T, GDN_HEADS, GDN_DK))
    va = va.reshape(B, T, GDN_HEADS, GDN_DV)
    beta = jax.nn.sigmoid(b_a.astype(jnp.float32))
    g = -jnp.exp(a_log.astype(jnp.float32)) * jax.nn.softplus(a_a.astype(jnp.float32) + dt_bias.astype(jnp.float32))
    oa = gated_delta_rule(qa, ka, va, g, beta)
    oa = rms_norm(oa, gdn_norm_w) * jax.nn.silu(za.reshape(B, T, GDN_HEADS, GDN_DV))
    ya = oa.reshape(B, T, GDN_V_W) @ w_o_a

    ob = swa_sink_attention(qb.reshape(B, T, SWA_HEADS, SWA_HEAD_DIM),
                            kb.reshape(B, T, SWA_KV_HEADS, SWA_HEAD_DIM),
                            vb.reshape(B, T, SWA_KV_HEADS, SWA_HEAD_DIM),
                            attn_sinks, pos_bias)
    ob = ob.reshape(B, T, SWA_Q_W) * jax.nn.silu(zb)
    yb = ob @ w_o_b

    merged = jax.nn.sigmoid(gate_a) * ya + jax.nn.sigmoid(gate_b) * yb
    return x + merged @ w_out

def setup_inputs(seed: int = 0) -> dict:
    key = jax.random.key(seed)
    ks = jax.random.split(key, 14)
    f32 = jnp.float32
    nrm = jax.random.normal
    x = nrm(ks[0], (BATCH, SEQ, D_MODEL), f32)
    norm_w = 1.0 + 0.02 * nrm(ks[1], (DEPTH, D_MODEL), f32)
    w_in = nrm(ks[2], (DEPTH, D_MODEL, D_IN), f32) * D_MODEL ** -0.5
    conv_w = nrm(ks[3], (DEPTH, GDN_CONV, GDN_CONV_CH), f32) * GDN_CONV ** -0.5
    a_log = jnp.log(jax.random.uniform(ks[4], (DEPTH, GDN_HEADS), f32, minval=1.0, maxval=16.0))
    dt = jnp.exp(jax.random.uniform(ks[5], (DEPTH, GDN_HEADS), f32,
                                    minval=math.log(1e-3), maxval=math.log(1e-1)))
    dt_bias = dt + jnp.log(-jnp.expm1(-dt))
    gdn_norm_w = 1.0 + 0.02 * nrm(ks[6], (DEPTH, GDN_DV), f32)
    attn_sinks = nrm(ks[7], (DEPTH, SWA_HEADS), f32)
    w_o_a = nrm(ks[8], (DEPTH, GDN_V_W, D_MODEL), f32) * GDN_V_W ** -0.5
    w_o_b = nrm(ks[9], (DEPTH, SWA_Q_W, D_MODEL), f32) * SWA_Q_W ** -0.5
    w_out = nrm(ks[10], (DEPTH, D_MODEL, D_MODEL), f32) * D_MODEL ** -0.5
    rel_bias = 0.5 * nrm(ks[11], (REL_BUCKETS, SWA_HEADS), f32)
    final_norm_w = 1.0 + 0.02 * nrm(ks[12], (D_MODEL,), f32)
    return {"x": x, "norm_w": norm_w, "w_in": w_in, "conv_w": conv_w, "a_log": a_log,
            "dt_bias": dt_bias, "gdn_norm_w": gdn_norm_w, "attn_sinks": attn_sinks,
            "w_o_a": w_o_a, "w_o_b": w_o_b, "w_out": w_out, "rel_bias": rel_bias,
            "final_norm_w": final_norm_w}

def reference(x, norm_w, w_in, conv_w, a_log, dt_bias, gdn_norm_w, attn_sinks,
              w_o_a, w_o_b, w_out, rel_bias, final_norm_w):
    pos_bias = banded_relative_bias(rel_bias)
    for layer in range(DEPTH):
        x = hybrid_layer(x, norm_w[layer], w_in[layer], conv_w[layer], a_log[layer], dt_bias[layer],
                         gdn_norm_w[layer], attn_sinks[layer], w_o_a[layer], w_o_b[layer],
                         w_out[layer], pos_bias)
    return rms_norm(x, final_norm_w)


_drawn_inputs = setup_inputs


def setup_inputs(seed=0):
    import zlib

    import numpy as np

    out = dict(_drawn_inputs(seed))
    spreads = {}
    factors = {'norm_w': 4.999, 'gdn_norm_w': 8.0, 'attn_sinks': 8.0, 'final_norm_w': 2.887}
    for name, (base, spread) in spreads.items():
        noise = np.random.default_rng([zlib.crc32(name.encode()), seed]).standard_normal(out[name].shape)
        drawn = base * np.exp(spread * noise) if base else spread * noise
        out[name] = __import__('jax').numpy.asarray(drawn.astype(out[name].dtype))
    for name, factor in factors.items():
        out[name] = (out[name] * factor).astype(out[name].dtype)
    return out
```

```python
from contextlib import ExitStack

import numpy as np
import concourse.bass as bass
from concourse import mybir

P = 128
D = 1024
KT = D // P
SEQ = 2048
TB = 512
NB = SEQ // TB
NT = TB // P
H = 8
CH = 64
NC = TB // CH
DH = 64
CONV = 4
TILE = KT * P
EPS = 1e-6
NEG = -3.0e38
LEVELS = 6

HEAD_TILES = 6
PRO_TILES = 4
GATE_TILES = 4
OUT_TILES = 8
TILES = PRO_TILES + H * HEAD_TILES + H * GATE_TILES + OUT_TILES
PAIRS = TILES // 2
EVACS = (TILES - OUT_TILES) // 2

F32 = mybir.dt.float32
F32R = mybir.dt.float32r
ALU = mybir.AluOpType
ACT = mybir.ActivationFunctionType
AX = mybir.AxisListType.X

IDENT, UPTO, AFTER, NEGSTRICT, ONES = range(5)
G, BETA, EGC, EGL, ETAIL = range(5)


class Chain:

    def __init__(self, eng, sem, base):
        self.eng, self.sem, self.base, self.k = eng, sem, base, 0

    def inc(self, ins):
        self.k += 1
        ins.then_inc(self.sem, 1)

    def sync(self):
        self.eng.wait_ge(self.sem, self.base + self.k)

    def link(self, ins):
        self.inc(ins)
        self.sync()


def build_program(nc, x, w_tiles, norm_w, gdn_norm_w, decay_bias, step_const, bias, final_w, masks, out):
    with ExitStack() as ctx:
        def sb(name, shape, dt=F32):
            return ctx.enter_context(nc.sbuf_tensor(name, shape, dt))

        def sem(name, n=None):
            if n is None:
                return ctx.enter_context(nc.semaphore(name))
            return [ctx.enter_context(nc.semaphore(f"{name}{i}")) for i in range(n)]

        hT_hi = sb("hT_hi", [P, KT, TB], F32R)
        hT_lo = sb("hT_lo", [P, KT, TB], F32R)
        oa_hi = sb("oa_hi", [P, H, TB], F32R)
        oa_lo = sb("oa_lo", [P, H, TB], F32R)
        ob_hi = sb("ob_hi", [P, H, TB], F32R)
        ob_lo = sb("ob_lo", [P, H, TB], F32R)
        w_raw = sb("w_raw", [P, 2, TILE])
        w_hi = sb("w_hi", [P, 2, TILE], F32R)
        w_lo = sb("w_lo", [P, 2, TILE], F32R)
        area1 = sb("area1", [P, 8 * TB])
        area2 = sb("area2", [P, 15 * TB])
        kb = sb("kb", [P, CH + TB])
        vb = sb("vb", [P, CH + TB])
        vwin = sb("vwin", [P, NC, P])
        zraw = sb("zraw", [P, 3, CONV - 1 + TB])
        hist = sb("hist", [P, H, 3, CONV - 1])
        za = sb("za", [P, 2, TB])
        zb = sb("zb", [P, 2, TB])
        qbd = sb("qbd", [P, 2, NC, P])
        s_all = sb("s_all", [P, H, P])
        s_cur = sb("s_cur", [P, 2, P])
        r_sb = sb("r_sb", [P, P])
        y_sb = sb("y_sb", [P, 2, P])
        mk = sb("mk", [P, 5, P])
        fw = sb("fw", [P, D])
        bias_sb = sb("bias_sb", [P, 2, 2, P])
        stc = sb("stc", [P, 2, 3 * CONV + 1])
        nw = sb("nw", [P, KT])
        gnw = sb("gnw", [P, 1])
        db = sb("db", [P, 2, H])
        nea = sb("nea", [P, H])
        ba = sb("ba", [P, NT, 2 * H])
        pa = sb("pa", [P, 6, NT, H])
        sc_all = sb("sc_all", [P, 5, NT, H])
        sc = sb("sc", [P, 5, NT])
        half = sb("half", [P, 8])
        st4 = sb("st4", [P, 12])
        ssq = sb("ssq", [P, 8])
        ssqe = sb("ssqe", [P, 8])
        rn = sb("rn", [P, 8])
        kn = sb("kn", [P, NT])
        rk2 = sb("rk2", [P, NT])
        bj = sb("bj", [P, NT])
        negc = sb("negc", [P, NT])
        ksc = sb("ksc", [P, NT])
        rqs = sb("rqs", [P, NT])
        sso = sb("sso", [P, NT])
        mso = sb("mso", [P, NT])
        rso = sb("rso", [P, NT])
        fo = sb("fo", [P, NT])
        mx = sb("mx", [P, NT])
        nmx = sb("nmx", [P, NT])
        psum_row = sb("psum_row", [P, NT])
        esink = sb("esink", [P, NT])
        den = sb("den", [P, NT])
        rden = sb("rden", [P, NT])

        x_sb = area1[:, :].rearrange("p (t c) -> p t c", t=NT)
        merged = area1[:, :].rearrange("p (c t) -> p c t", c=KT)
        qkv = area1[:, 0:6 * TB].rearrange("p (r i t) -> p r i t", r=2, i=3)

        def scratch(i, n=1):
            return area2[:, i * TB:(i + n) * TB]

        def chunks(ap):
            return ap.rearrange("p (t c) -> p t c", t=NT)

        g_up = chunks(scratch(0))
        dec = chunks(scratch(1))
        b_up = chunks(scratch(2))
        dec_n = chunks(scratch(3))
        p_sb = [chunks(scratch(4)), chunks(scratch(5))]
        pt_sb = [chunks(scratch(6)), chunks(scratch(7))]
        tt_sb = [chunks(scratch(8)), chunks(scratch(9))]
        attn = chunks(scratch(10))
        kd = chunks(scratch(11))
        vr = chunks(scratch(12))
        o_sb = chunks(scratch(13))
        o1_sb = chunks(scratch(14))
        junk = scratch(0)
        lg = p_sb[0]
        pts = pt_sb[0]
        oa32 = scratch(5)
        ob32 = scratch(7)
        y_out = area2[:, 0:8 * TB].rearrange("p (t c) -> p t c", t=NT)
        junk2 = area2[:, 8 * TB:10 * TB]
        h32 = [scratch(10), scratch(11)]
        ba_t = scratch(12)
        ga = scratch(0)
        gb = scratch(1)
        ma = scratch(2)
        mb = scratch(3)

        bank = [ctx.enter_context(nc.psum_tensor(f"bank{i}", [P, TB], F32)) for i in range(8)]

        def bch(i):
            return bank[i][:, :].rearrange("p (t c) -> p t c", t=NT)

        const_in = sem("const_in")
        zeroed = sem("zeroed")
        const_ready = sem("const_ready")
        w_landed = sem("w_landed", 2)
        hi_ready = sem("hi_ready", 2)
        lo_ready = sem("lo_ready", 2)
        gemm_done = sem("gemm_done", 2)
        z_read = sem("z_read", 2)
        x_landed = sem("x_landed")
        x_ssq = sem("x_ssq")
        x_mean = sem("x_mean")
        x_rstd = sem("x_rstd")
        x_normed = sem("x_normed")
        xt_done = sem("xt_done", 2)
        h32_ready = sem("h32_ready", 2)
        h_hi = sem("h_hi", 2)
        h_lo = sem("h_lo", 2)
        kv_hist = sem("kv_hist")
        ba_done = sem("ba_done")
        ba_read = sem("ba_read")
        vwin_t = sem("vwin_t", 2)
        vwin_ready = sem("vwin_ready")
        pre_exp = sem("pre_exp")
        exps = sem("exps")
        sp_in = sem("sp_in")
        lns = sem("lns")
        g_ready = sem("g_ready")
        cums = sem("cums")
        ecums = sem("ecums")
        step_in = sem("step_in")
        conv_ready = sem("conv_ready", 3)
        zraw_free = sem("zraw_free")
        act_q = sem("act_q", 3)
        za_ready = sem("za_ready")
        qbd_ready = sem("qbd_ready")
        zb_ready = sem("zb_ready")
        head_dve_done = sem("head_dve_done")
        sc_ready = sem("sc_ready")
        gup_ready = sem("gup_ready")
        tr_done = sem("tr_done", 3)
        dec_done = sem("dec_done")
        kk_done = sem("kk_done")
        qk_done = sem("qk_done")
        ssq_ready = sem("ssq_ready")
        ssqe_ready = sem("ssqe_ready")
        rn_ready = sem("rn_ready")
        b_ready = sem("b_ready")
        ksc_ready = sem("ksc_ready")
        kd_ready = sem("kd_ready")
        vr_ready = sem("vr_ready")
        dec_ready = sem("dec_ready")
        bup_ready = sem("bup_ready")
        decn_in = sem("decn_in")
        decn_ready = sem("decn_ready")
        attn_ready = sem("attn_ready")
        p_done = sem("p_done")
        pt_done = sem("pt_done")
        tt_done = sem("tt_done")
        p_ready = sem("p_ready")
        pt_ready = sem("pt_ready")
        tt_ready = sem("tt_ready")
        s0_ready = sem("s0_ready")
        ks_done = sem("ks_done")
        qs_done = sem("qs_done")
        r_ready = sem("r_ready")
        y_done = sem("y_done")
        y_ready = sem("y_ready")
        ds_done = sem("ds_done")
        ay_done = sem("ay_done")
        s_ready = sem("s_ready")
        o1_ready = sem("o1_ready")
        o_ready = sem("o_ready")
        sso_ready = sem("sso_ready")
        mso_ready = sem("mso_ready")
        rso_ready = sem("rso_ready")
        on_ready = sem("on_ready")
        ot_done = sem("ot_done")
        lg_done = sem("lg_done", 2)
        nmx_ready = sem("nmx_ready", 2)
        exp_ready = sem("exp_ready", 2)
        prob_ready = sem("prob_ready", 2)
        prt_done = sem("prt_done", 2)
        pts_ready = sem("pts_ready", 2)
        pv_done = sem("pv_done", 2)
        pv_read = sem("pv_read", 2)
        merged_ready = sem("merged_ready")
        m_hi = sem("m_hi", KT)
        m_lo = sem("m_lo", KT)
        x2_landed = sem("x2_landed")
        res_ready = sem("res_ready")
        y_ssq = sem("y_ssq")
        y_mean = sem("y_mean")
        y_rstd = sem("y_rstd")
        y_ready2 = sem("y_final")
        y_stored = sem("y_stored")
        dve_init, dve_pro, dve_proj, dve_head = sem("dve_init"), sem("dve_pro"), sem("dve_proj"), sem("dve_head")
        act_pro, act_head = sem("act_pro"), sem("act_head")
        DVE_PRO, DVE_HEAD, DVE_PROJ, ACT_PRO, ACT_HEAD = 12, 20, 10, 3, 1

        block = ctx.enter_context(nc.Block())

        @block.sync
        def _(sp):
            for s in range(2):
                sp.dma_start(w_raw[:, s, :], w_tiles[s]).then_inc(w_landed[s], 16)
            with sp.Fori(0, NB) as b:
                with sp.Fori(0, PAIRS) as u:
                    used = sp.snap(b * PAIRS + u + 1)
                    for s in range(2):
                        sp.wait_ge(hi_ready[s], used)
                        sp.wait_ge(lo_ready[s], used)
                        sp.dma_start(w_raw[:, s, :], w_tiles[bass.ds(u * 2 + (2 + s), 1)].rearrange("o p n -> p (o n)")
                                     ).then_inc(w_landed[s], 16)

        @block.gpsimd
        def _(pool):
            pool.memset(kb[:, :], 0.0).then_inc(zeroed, 1)
            pool.memset(vb[:, :], 0.0).then_inc(zeroed, 1)
            pool.memset(qbd[:, :, :, :], 0.0).then_inc(zeroed, 1)
            pool.memset(s_all[:, :, :], 0.0).then_inc(zeroed, 1)
            pool.memset(hist[:, :, :, :], 0.0).then_inc(zeroed, 1)
            pool.memset(half[:, :], -0.5).then_inc(zeroed, 1)
            for i, s in enumerate((*z_read, zraw_free, head_dve_done, ot_done, merged_ready, y_stored)):
                pool.memset(st4[:, i:i + 1], 0.0).then_inc(s, 1)
            pool.wait_ge(zeroed, 6)
            pool.wait_ge(const_in, 16 * 6)

            def low_part(s, n):
                pool.wait_ge(hi_ready[s], n)
                pool.tensor_tensor(w_lo[:, s, :], w_raw[:, s, :], w_hi[:, s, :].bitcast(F32),
                                   ALU.subtract).then_inc(lo_ready[s], 1)

            def power(dst, src, n, src_ready, value, ready):
                pool.wait_ge(src_ready, value)
                pool.tensor_tensor(dst, src, half[:, 0:n], ALU.pow).then_inc(ready, 1)

            for s in range(2):
                low_part(s, 1)
            with pool.Fori(0, NB) as b:
                b1 = pool.snap(b + 1)
                ub = pool.snap(b * PAIRS)
                power(st4[:, 4:8], st4[:, 8:12], NT, x_mean, b1, x_rstd)
                for k in range(PRO_TILES):
                    low_part(k % 2, ub + (k // 2 + 2))
                with pool.Fori(0, H) as h:
                    n1 = pool.snap(b * H + h + 1)
                    u = pool.snap(b * PAIRS + h * (HEAD_TILES // 2) + PRO_TILES // 2)
                    for k in range(HEAD_TILES):
                        low_part(k % 2, u + (k // 2 + 2))
                    pool.wait_ge(sc_ready, n1)
                    pool.tensor_tensor(g_up, mk[:, UPTO:UPTO + 1, :].to_broadcast([P, NT, P]),
                                       sc[:, G, :, None].to_broadcast([P, NT, P]), ALU.mult).then_inc(gup_ready, 1)
                    power(rn[:, :], ssqe[:, :], 8, ssqe_ready, n1, rn_ready)
                    pool.wait_ge(b_ready, n1)
                    pool.tensor_tensor(b_up, mk[:, UPTO:UPTO + 1, :].to_broadcast([P, NT, P]),
                                       bj[:, :, None].to_broadcast([P, NT, P]), ALU.mult).then_inc(bup_ready, 1)
                    pool.wait_ge(decn_in, n1)
                    pool.tensor_tensor(dec_n, dec, mk[:, NEGSTRICT:NEGSTRICT + 1, :].to_broadcast([P, NT, P]),
                                       ALU.mult).then_inc(decn_ready, 1)
                    power(rso[:, :], mso[:, :], NT, mso_ready, n1, rso_ready)
                with pool.Fori(0, H) as c:
                    u = pool.snap(b * PAIRS + c * (GATE_TILES // 2) + (PRO_TILES + H * HEAD_TILES) // 2)
                    for k in range(GATE_TILES):
                        low_part(k % 2, u + (k // 2 + 2))
                for k in range(OUT_TILES):
                    low_part(k % 2, ub + (PAIRS - OUT_TILES // 2 + k // 2 + 2))
                power(st4[:, 4:8], st4[:, 8:12], NT, y_mean, b1, y_rstd)

        @block.scalar
        def _(act):
            act.dma_start(mk[:, :, :], masks).then_inc(const_in, 16)
            act.dma_start(fw[:, :], final_w).then_inc(const_in, 16)
            act.dma_start(nw[:, :], norm_w).then_inc(const_in, 16)
            act.dma_start(gnw[:, :], gdn_norm_w).then_inc(const_in, 16)
            act.dma_start(db[:, :, :], decay_bias).then_inc(const_in, 16)
            act.dma_start(bias_sb[:, 0, :, :], bias[0]).then_inc(const_in, 16)

            def high_part(s, n, n16):
                act.wait_ge(w_landed[s], n16)
                act.activation(w_hi[:, s, :], w_raw[:, s, :], ACT.Copy).then_inc(hi_ready[s], 1)

            def product(s, n, n16):
                act.wait_ge(gemm_done[s], n)
                high_part(s, n + 1, n16 + 16)

            for s in range(2):
                high_part(s, 1, 16)
            act.wait_ge(const_in, 16 * 6)
            act.wait_ge(zeroed, 6)
            act.activation(nea[:, :], db[:, 0, :], ACT.Exp).then_inc(const_ready, 1)
            with act.Fori(0, NB) as b:
                b1 = act.snap(b + 1)
                ub = act.snap(b * PAIRS + 1)
                ub16 = act.snap(b * (PAIRS * 16) + 16)
                ch = Chain(act, act_pro, act.snap(b * ACT_PRO))
                act.wait_ge(y_stored, b * 16 + 1)
                act.dma_start(x_sb, x[bass.ds(b, 1)].rearrange("o p t c -> p (o t) c")).then_inc(x_landed, 16)
                act.wait_ge(x_landed, b1 * 16)
                for t in range(NT):
                    act.activation(junk2, x_sb[:, t, :], ACT.Square, accum_out=st4[:, t:t + 1]).then_inc(x_ssq, 1)
                    act.wait_ge(x_ssq, b * NT + (t + 1))
                for k in range(KT):
                    r = k % 2
                    act.wait_ge(h32_ready[r], b * (KT // 2) + (k // 2 + 1))
                    act.activation(hT_hi[:, k, :], h32[r], ACT.Copy).then_inc(h_hi[r], 1)
                ch.inc(act.activation(kb[:, 0:CH], kb[:, TB:TB + CH], ACT.Copy))
                ch.link(act.activation(vb[:, 0:CH], vb[:, TB:TB + CH], ACT.Copy))
                for k, dst in enumerate((kb, vb)):
                    product(k, ub, ub16)
                    act.activation(dst[:, CH:CH + TB], bank[k][:, :], ACT.Copy).then_inc(z_read[k], 1)
                product(0, ub + 1, ub16 + 16)
                act.activation(ba_t, bank[0][:, :], ACT.Copy).then_inc(z_read[0], 1)
                product(1, ub + 1, ub16 + 16)
                act.activation(st4[:, 0:1], bank[1][:, 0:1], ACT.Copy).then_inc(z_read[1], 1)
                for v in range(2):
                    act.wait_ge(vwin_t[v], b1)
                    act.activation(vwin[:, v * NT:(v + 1) * NT, :], bch(2 + v), ACT.Copy).then_inc(vwin_ready, 1)
                act.wait_ge(pre_exp, b1)
                ch.inc(act.activation(pa[:, 2, :, :], ba[:, :, 0:H], ACT.Exp, scale=-1.0))
                act.activation(pa[:, 3, :, :], pa[:, 1, :, :], ACT.Exp).then_inc(exps, 1)
                act.wait_ge(sp_in, b1)
                act.activation(pa[:, 1, :, :], pa[:, 4, :, :], ACT.Ln).then_inc(lns, 1)
                act.wait_ge(cums, b1)
                act.activation(sc_all[:, EGC:ETAIL + 1, :, :].rearrange("p q t h -> p (q t h)"),
                               bank[5][:, 0:3 * NT * H], ACT.Exp).then_inc(ecums, 1)
                assert ch.k == ACT_PRO

                def project(par, n1, u, u16):
                    nonlocal_n = n1
                    act.wait_ge(head_dve_done, n1)
                    act.wait_ge(ot_done, n1)
                    act.dma_start(stc[:, par, :], step_const[bass.ds(hh, 1)].rearrange("o p n -> p (o n)")
                                  ).then_inc(step_in, 16)
                    act.dma_start(bias_sb[:, par, :, :], bias[bass.ds(nonlocal_n - 1, 1)].rearrange("o p a n -> p (o a) n")
                                  ).then_inc(step_in, 16)
                    act.wait_ge(zraw_free, n1)
                    for i in range(3):
                        product(i % 2, u + i // 2, u16 + (i // 2) * 16)
                        act.activation(zraw[:, i, CONV - 1:], bank[i % 2][:, :], ACT.Copy).then_inc(z_read[i % 2], 1)
                    product(1, u + 1, u16 + 16)
                    act.activation(za[:, par, :], bank[1][:, :], ACT.Silu).then_inc(z_read[1], 1)
                    product(0, u + 2, u16 + 32)
                    zq = bank[0][:, :].rearrange("p (c t) -> p c t", c=NC)
                    act.activation(qbd[0:DH, par, :, 0:CH], zq[0:DH], ACT.Copy, scale=DH ** -0.5)
                    act.activation(qbd[DH:P, par, :, CH:P], zq[DH:P], ACT.Copy, scale=DH ** -0.5).then_inc(z_read[0], 1)
                    product(1, u + 2, u16 + 32)
                    act.activation(zb[:, par, :], bank[1][:, :], ACT.Silu).then_inc(z_read[1], 1)
                    for i in range(3):
                        act.wait_ge(conv_ready[i], n1)
                        act.activation(qkv[:, par, i, :], qkv[:, par, i, :], ACT.Silu).then_inc(act_q[i], 1)

                def head(par, n1):
                    n4, n5, n7 = (act.snap((n1 - 1) * i) for i in (NT, LEVELS - 1, LEVELS + 1))
                    ch = Chain(act, act_head, act.snap((n1 - 1) * ACT_HEAD))
                    for i in range(2):
                        act.wait_ge(tr_done[i], n1)
                        for t in range(NT):
                            ins = act.activation(o1_sb[:, t, :], bch(2 + i)[:, t, :], ACT.Square,
                                                 accum_out=ssq[:, i * NT + t:i * NT + t + 1])
                            if (i, t) == (1, NT - 1):
                                ins.then_inc(ssq_ready, 1)
                            elif t == NT - 1:
                                ch.link(ins)
                    act.wait_ge(dec_done, n1)
                    act.activation(dec, bch(5), ACT.Exp).then_inc(dec_ready, 1)
                    act.wait_ge(ksc_ready, n1)
                    for t in range(NT):
                        ins = act.activation(kd[:, t, :], bch(3)[:, t, :], ACT.Copy, scale=ksc[:, t:t + 1])
                        if t == NT - 1:
                            ins.then_inc(kd_ready, 1)
                    act.wait_ge(tr_done[2], n1)
                    for t in range(NT):
                        ins = act.activation(vr[:, t, :], bch(4)[:, t, :], ACT.Copy, scale=kn[:, t:t + 1])
                        if t == NT - 1:
                            ins.then_inc(vr_ready, 1)
                    for l in range(LEVELS + 1):
                        act.wait_ge(p_done, n7 + (l + 1))
                        act.activation(p_sb[l % 2], bch(5), ACT.Copy).then_inc(p_ready, 1)
                        if 1 <= l < LEVELS:
                            act.wait_ge(pt_done, n5 + l)
                            if l == 2:
                                act.wait_ge(tt_ready, n7 + 1)
                            act.activation(pt_sb[l % 2], bch(3), ACT.Copy).then_inc(pt_ready, 1)
                    for t in range(NT):
                        act.wait_ge(qs_done, n4 + (t + 1))
                        act.activation(o1_sb[:, t, :], bank[2][:, 0:P], ACT.Copy, scale=sc[:, EGC, t:t + 1]
                                       ).then_inc(o1_ready, 1)
                        act.wait_ge(y_done, n4 + (t + 1))
                        act.activation(y_sb[:, t % 2, :], bank[6][:, 0:P], ACT.Copy).then_inc(y_ready, 1)
                    for t in range(NT):
                        act.wait_ge(o_ready, n4 + (t + 1))
                        ins = act.activation(g_up[:, t, :], o_sb[:, t, :], ACT.Square, accum_out=sso[:, t:t + 1])
                        if t == NT - 1:
                            ins.then_inc(sso_ready, 1)
                    sink = stc[:, par, 3 * CONV:3 * CONV + 1]
                    for g in range(2):
                        act.wait_ge(nmx_ready[g], n1)
                        for t in range(NT):
                            act.activation(lg[:, t, :], lg[:, t, :], ACT.Exp, bias=nmx[:, t:t + 1],
                                           accum_out=psum_row[:, t:t + 1])
                        act.activation(esink[:, :], nmx[:, :], ACT.Exp, bias=sink).then_inc(exp_ready[g], 1)
                        act.wait_ge(prt_done[g], n1)
                        act.activation(pts, bch(5), ACT.Copy).then_inc(pts_ready[g], 1)
                    assert ch.k == ACT_HEAD, ch.k

                with act.Fori(0, H // 2) as hp:
                    for par in range(2):
                        n1 = act.snap(b * H + hp * 2 + (par + 1))
                        hh = act.snap(hp * 2 + par)
                        u = act.snap(b * PAIRS + hp * HEAD_TILES + (PRO_TILES // 2 + par * HEAD_TILES // 2 + 1))
                        u16 = act.snap(u * 16)
                        project(par, n1, u, u16)
                        head(par, n1)

                with act.Fori(0, KT) as c:
                    u = act.snap(b * PAIRS + c * 2 + ((PRO_TILES + H * HEAD_TILES) // 2 + 1))
                    u16 = act.snap(u * 16)
                    v = act.snap(b * EVACS + c * 2 + ((PRO_TILES + H * HEAD_TILES) // 2 + 1))
                    product(0, u, u16)
                    act.wait_ge(z_read[1], v)
                    act.activation(ga, bank[0][:, :], ACT.Sigmoid).then_inc(z_read[0], 1)
                    product(1, u, u16)
                    product(0, u + 1, u16 + 16)
                    act.activation(gb, bank[0][:, :], ACT.Sigmoid).then_inc(z_read[0], 1)
                    product(1, u + 1, u16 + 16)

                act.wait_ge(merged_ready, b1 * KT + 1)
                act.dma_start(y_out, x[bass.ds(b, 1)].rearrange("o p t c -> p (o t) c")).then_inc(x2_landed, 16)
                for k in range(KT):
                    act.activation(hT_hi[:, k, :], merged[:, k, :], ACT.Copy).then_inc(m_hi[k], 1)
                for k in range(OUT_TILES):
                    product(k % 2, ub + (PAIRS - OUT_TILES // 2 + k // 2), ub16 + (PAIRS - OUT_TILES // 2 + k // 2) * 16)
                act.wait_ge(res_ready, b1)
                for t in range(NT):
                    act.activation(junk2, y_out[:, t, :], ACT.Square, accum_out=st4[:, t:t + 1]).then_inc(y_ssq, 1)
                    act.wait_ge(y_ssq, b * NT + (t + 1))
                act.wait_ge(y_ready2, b1)
                act.dma_start(out[bass.ds(b, 1)].rearrange("o p t c -> p (o t) c"), y_out).then_inc(y_stored, 16)
            act.wait_ge(y_stored, NB * 16 + 1)

        @block.vector
        def _(dve):
            dve.wait_ge(const_in, 16 * 6)
            dve.wait_ge(zeroed, 6)
            dve.wait_ge(const_ready, 1)

            def copy(dst, src):
                return dve.tensor_scalar(dst, src, 1.0, None, ALU.mult)

            dve.tensor_scalar(nea[:, :], nea[:, :], -1.0, None, ALU.mult).then_inc(dve_init, 1)
            dve.wait_ge(dve_init, 1)
            with dve.Fori(0, NB) as b:
                b1 = dve.snap(b + 1)
                ch = Chain(dve, dve_pro, dve.snap(b * DVE_PRO))
                dve.wait_ge(x_ssq, b1 * NT)
                dve.tensor_scalar(st4[:, 8:12], st4[:, 0:4], 1.0 / D, EPS, ALU.mult, ALU.add).then_inc(x_mean, 1)
                dve.wait_ge(x_rstd, b1)
                for t in range(NT):
                    ins = dve.tensor_scalar(x_sb[:, t, :], x_sb[:, t, :], st4[:, 4 + t:5 + t], None, ALU.mult)
                ins.then_inc(x_normed, 1)
                for k in range(KT):
                    r = k % 2
                    kk = b * (KT // 2) + (k // 2 + 1)
                    dve.wait_ge(xt_done[r], kk)
                    if k >= 2:
                        dve.wait_ge(h_lo[r], kk - 1)
                    dve.tensor_scalar(h32[r], bank[r][:, :], nw[:, k:k + 1], None, ALU.mult).then_inc(h32_ready[r], 1)
                    dve.wait_ge(h_hi[r], kk)
                    dve.tensor_tensor(hT_lo[:, k, :], h32[r], hT_hi[:, k, :].bitcast(F32), ALU.subtract).then_inc(h_lo[r], 1)
                dve.wait_ge(ba_done, b1)
                ch.inc(dve.tensor_copy(ba[:, :, :], bch(4)[:, :, 0:2 * H]))
                ch.sync()
                y = pa[:, 0, :, :]
                ch.link(dve.tensor_tensor(y, ba[:, :, H:2 * H], db[:, 1:2, :].to_broadcast([P, NT, H]), ALU.add))
                ch.link(dve.tensor_scalar(pa[:, 1, :, :], y, -1.0, None, ALU.mult))
                dve.tensor_tensor(pa[:, 1, :, :], pa[:, 1, :, :], y, ALU.min).then_inc(pre_exp, 1)
                dve.wait_ge(exps, b1)
                e, w = pa[:, 3, :, :], pa[:, 4, :, :]
                dve.tensor_scalar(w, e, 1.0, None, ALU.add).then_inc(sp_in, 1)
                dve.wait_ge(sp_in, b1)
                ch.link(dve.tensor_scalar(pa[:, 5, :, :], w, -1.0, None, ALU.add))
                ch.link(dve.tensor_tensor(e, e, pa[:, 5, :, :], ALU.subtract))
                ch.link(dve.reciprocal(pa[:, 5, :, :], w))
                ch.link(dve.tensor_tensor(e, e, pa[:, 5, :, :], ALU.mult))
                ch.link(dve.tensor_scalar(y, y, 0.0, None, ALU.max))
                ch.link(dve.tensor_tensor(y, y, e, ALU.add))
                ch.link(dve.tensor_scalar(pa[:, 2, :, :], pa[:, 2, :, :], 1.0, None, ALU.add))
                ch.link(dve.reciprocal(sc_all[:, BETA, :, :], pa[:, 2, :, :]))
                dve.wait_ge(lns, b1)
                ch.link(dve.tensor_tensor(y, y, pa[:, 1, :, :], ALU.add))
                dve.tensor_tensor(sc_all[:, G, :, :], y, nea[:, None, :].to_broadcast([P, NT, H]), ALU.mult).then_inc(g_ready, 1)
                assert ch.k == DVE_PRO, ch.k

                def project(par, n1, v):
                    ch = Chain(dve, dve_proj, dve.snap((n1 - 1) * DVE_PROJ))
                    ch.link(copy(zraw[:, :, 0:CONV - 1], hist[:, bass.ds(hh, 1), :, :].rearrange("p o i n -> p (o i) n")))
                    dve.wait_ge(step_in, n1 * 32)
                    dve.wait_ge(ot_done, n1)
                    for i in range(3):
                        dve.wait_ge(z_read[i % 2], v + i // 2)
                        acc = qkv[:, par, i, :]
                        ch.link(dve.tensor_scalar(acc, zraw[:, i, 0:TB], stc[:, par, CONV * i:CONV * i + 1], None, ALU.mult))
                        for k in range(1, CONV):
                            ins = dve.scalar_tensor_tensor(acc, zraw[:, i, k:k + TB], stc[:, par, CONV * i + k:CONV * i + k + 1],
                                                           acc, ALU.mult, ALU.add)
                            if k < CONV - 1:
                                ch.link(ins)
                            else:
                                ins.then_inc(conv_ready[i], 1)
                    copy(hist[:, bass.ds(hh, 1), :, :].rearrange("p o i n -> p (o i) n"), zraw[:, :, TB:TB + CONV - 1]
                                    ).then_inc(zraw_free, 1)
                    dve.wait_ge(zraw_free, n1 + 1)
                    assert ch.k == DVE_PROJ, ch.k

                def head(par, n1):
                    n4, n6, n7 = (dve.snap((n1 - 1) * i) for i in (NT, LEVELS, LEVELS + 1))
                    ch = Chain(dve, dve_head, dve.snap((n1 - 1) * DVE_HEAD))
                    dve.wait_ge(ecums, b1)
                    copy(sc[:, :, :], sc_all[:, :, :, bass.ds(hh, 1)].rearrange("p q t o -> p q (t o)")).then_inc(sc_ready, 1)
                    copy(s_cur[:, 0, :], s_all[:, bass.ds(hh, 1), :].rearrange("p o c -> p (o c)")).then_inc(s0_ready, 1)
                    dve.wait_ge(ssq_ready, n1)
                    dve.tensor_scalar(ssqe[:, :], ssq[:, :], EPS, None, ALU.add).then_inc(ssqe_ready, 1)
                    dve.wait_ge(sc_ready, n1)
                    dve.tensor_scalar(negc[:, :], sc[:, EGC, :], -1.0, None, ALU.mult)
                    dve.wait_ge(rn_ready, n1)
                    ch.inc(dve.tensor_tensor(kn[:, :], rn[:, NT:8], ssqe[:, NT:8], ALU.mult))
                    ch.inc(dve.tensor_scalar(rqs[:, :], rn[:, 0:NT], float(P) ** -0.5, None, ALU.mult))
                    ch.link(dve.tensor_tensor(rk2[:, :], rn[:, NT:8], rn[:, NT:8], ALU.mult))
                    dve.tensor_tensor(bj[:, :], rk2[:, :], sc[:, BETA, :], ALU.mult).then_inc(b_ready, 1)
                    dve.wait_ge(b_ready, n1)
                    dve.tensor_tensor(ksc[:, :], bj[:, :], sc[:, ETAIL, :], ALU.mult).then_inc(ksc_ready, 1)
                    dve.wait_ge(dec_ready, n1)
                    dve.wait_ge(bup_ready, n1)
                    dve.tensor_tensor(dec, dec, b_up, ALU.mult).then_inc(decn_in, 1)
                    dve.wait_ge(decn_in, n1)
                    dve.wait_ge(qk_done, n1)
                    dve.tensor_tensor(attn, bch(7), dec, ALU.mult).then_inc(attn_ready, 1)
                    dve.wait_ge(decn_ready, n1)
                    dve.tensor_tensor(pt_sb[0], bch(6), dec_n, ALU.mult).then_inc(pt_ready, 1)
                    dve.wait_ge(pt_ready, n6 + 1)
                    dve.tensor_tensor(tt_sb[0], pt_sb[0], mk[:, IDENT:IDENT + 1, :].to_broadcast([P, NT, P]), ALU.add
                                      ).then_inc(tt_ready, 1)
                    for l in range(1, LEVELS + 1):
                        dve.wait_ge(tt_ready, n7 + l)
                        dve.wait_ge(tt_done, n6 + l)
                        dve.tensor_tensor(tt_sb[l % 2], bch(4), tt_sb[(l - 1) % 2], ALU.add).then_inc(tt_ready, 1)
                    dve.wait_ge(vr_ready, n1)
                    for t in range(NT):
                        dve.wait_ge(ks_done, n4 + (t + 1))
                        dve.scalar_tensor_tensor(r_sb[:, :], bank[6][:, 0:P], negc[:, t:t + 1], vr[:, t, :], ALU.mult, ALU.add
                                                 ).then_inc(r_ready, 1)
                        dve.wait_ge(s_ready if t else s0_ready, n4 + t if t else n1)
                        dve.wait_ge(ds_done, n4 + (t + 1))
                        dve.scalar_tensor_tensor(s_cur[:, (t + 1) % 2, :], s_cur[:, t % 2, :], sc[:, EGL, t:t + 1], bank[3][:, 0:P],
                                                 ALU.mult, ALU.add).then_inc(s_ready, 1)
                        dve.wait_ge(ay_done, n4 + (t + 1))
                        dve.wait_ge(o1_ready, n4 + (t + 1))
                        dve.tensor_tensor(o_sb[:, t, :], bank[7][:, 0:P], o1_sb[:, t, :], ALU.add).then_inc(o_ready, 1)
                    dve.wait_ge(s_ready, n4 + NT)
                    ch.inc(copy(s_all[:, bass.ds(hh, 1), :].rearrange("p o c -> p (o c)"), s_cur[:, 0, :]))
                    dve.wait_ge(sso_ready, n1)
                    ch.link(dve.tensor_tensor(mso[:, :], sso[:, :], rqs[:, :], ALU.mult))
                    ch.link(dve.tensor_tensor(mso[:, :], mso[:, :], rqs[:, :], ALU.mult))
                    dve.tensor_scalar(mso[:, :], mso[:, :], 1.0 / P, EPS, ALU.mult, ALU.add).then_inc(mso_ready, 1)
                    sink = stc[:, par, 3 * CONV:3 * CONV + 1]
                    for g in range(2):
                        dve.wait_ge(lg_done[g], n1)
                        if g:
                            dve.wait_ge(prt_done[0], n1)
                            ch.inc(dve.tensor_tensor(lg, bch(4), bias_sb[:, par, 1:2, :].to_broadcast([P, NT, P]), ALU.add))
                        else:
                            ch.inc(dve.tensor_tensor(lg[:, 0, :], bank[4][:, 0:P], bias_sb[:, par, 0, :], ALU.add))
                            ch.inc(dve.tensor_tensor(lg[:, 1:NT, :], bch(4)[:, 1:NT, :],
                                                     bias_sb[:, par, 1:2, :].to_broadcast([P, NT - 1, P]), ALU.add))
                        ch.sync()
                        ch.link(dve.tensor_reduce(mx[:, :], lg, AX, ALU.max))
                        dve.tensor_scalar(nmx[:, :], mx[:, :], sink, -1.0, ALU.max, ALU.mult).then_inc(nmx_ready[g], 1)
                        dve.wait_ge(exp_ready[g], n1)
                        ch.link(dve.tensor_tensor(den[:, :], psum_row[:, :], esink[:, :], ALU.add))
                        ch.link(dve.reciprocal(rden[:, :], den[:, :]))
                        dve.tensor_tensor(lg, lg, rden[:, :, None].to_broadcast([P, NT, P]), ALU.mult).then_inc(prob_ready[g], 1)
                        dve.wait_ge(pv_done[g], n1)
                        for lo, hi in ((0, CH), (CH, P)):
                            ins = dve.tensor_tensor(
                                ob32[lo:hi, g * NT * CH:(g + 1) * NT * CH].rearrange("p (u t) -> p u t", u=NT),
                                bch(4)[lo:hi, :, lo:hi],
                                zb[lo:hi, par, g * NT * CH:(g + 1) * NT * CH].rearrange("p (u t) -> p u t", u=NT), ALU.mult)
                        ins.then_inc(pv_read[g], 1)
                    dve.wait_ge(pv_read[1], n1)
                    obh = ob_hi[:, bass.ds(hh, 1), :].rearrange("p o t -> p (o t)")
                    ch.link(dve.tensor_scalar(obh, ob32, 1.0, None, ALU.mult))
                    ch.inc(dve.tensor_tensor(ob_lo[:, bass.ds(hh, 1), :].rearrange("p o t -> p (o t)"), ob32, obh.bitcast(F32), ALU.subtract))
                    dve.wait_ge(rso_ready, n1)
                    ch.link(dve.tensor_tensor(fo[:, :], rso[:, :], rqs[:, :], ALU.mult))
                    dve.tensor_tensor(o_sb, o_sb, fo[:, :, None].to_broadcast([P, NT, P]), ALU.mult).then_inc(on_ready, 1)
                    dve.wait_ge(ot_done, n1 + 1)
                    ch.link(dve.scalar_tensor_tensor(oa32, bank[2][:, :], gnw[:, 0:1], za[:, par, :], ALU.mult, ALU.mult))
                    oah = oa_hi[:, bass.ds(hh, 1), :].rearrange("p o t -> p (o t)")
                    ch.link(dve.tensor_scalar(oah, oa32, 1.0, None, ALU.mult))
                    dve.tensor_tensor(oa_lo[:, bass.ds(hh, 1), :].rearrange("p o t -> p (o t)"), oa32, oah.bitcast(F32), ALU.subtract
                                      ).then_inc(head_dve_done, 1)
                    assert ch.k == DVE_HEAD, ch.k

                with dve.Fori(0, H // 2) as hp:
                    for par in range(2):
                        n1 = dve.snap(b * H + hp * 2 + (par + 1))
                        hh = dve.snap(hp * 2 + par)
                        v = dve.snap(b * EVACS + hp * HEAD_TILES + (PRO_TILES // 2 + par * HEAD_TILES // 2 + 2))
                        project(par, n1, v)
                        head(par, n1)

                with dve.Fori(0, KT) as c:
                    v = dve.snap(b * EVACS + c * 2 + ((PRO_TILES + H * HEAD_TILES) // 2 + 2))
                    u = dve.snap(b * PAIRS + c * 2 + ((PRO_TILES + H * HEAD_TILES) // 2 + 1))
                    dve.wait_ge(z_read[0], v)
                    dve.wait_ge(merged_ready, b * KT + c + 1)
                    dve.wait_ge(gemm_done[1], u)
                    dve.tensor_tensor(ma, bank[1][:, :], ga, ALU.mult).then_inc(z_read[1], 1)
                    dve.wait_ge(z_read[1], v)
                    dve.wait_ge(z_read[0], v + 1)
                    dve.wait_ge(gemm_done[1], u + 1)
                    dve.tensor_tensor(mb, bank[1][:, :], gb, ALU.mult).then_inc(z_read[1], 1)
                    dve.wait_ge(z_read[1], v + 1)
                    dve.tensor_tensor(merged[:, bass.ds(c, 1), :].rearrange("p o t -> p (o t)"), ma, mb, ALU.add).then_inc(merged_ready, 1)

                for k in range(KT):
                    dve.wait_ge(m_hi[k], b1)
                    dve.tensor_tensor(hT_lo[:, k, :], merged[:, k, :], hT_hi[:, k, :].bitcast(F32), ALU.subtract).then_inc(m_lo[k], 1)
                dve.wait_ge(x2_landed, b1 * 16)
                for n in range(2):
                    for s in range(2):
                        dve.wait_ge(gemm_done[s], b1 * PAIRS + (n - 1) * 2)
                    for t in range(NT):
                        half_row = y_out[:, t, n * TB:(n + 1) * TB]
                        ins = dve.tensor_tensor(half_row, bank[OUT_BANKS[n][t]][:, :], half_row, ALU.add)
                ins.then_inc(res_ready, 1)
                dve.wait_ge(y_ssq, b1 * NT)
                dve.tensor_scalar(st4[:, 8:12], st4[:, 0:4], 1.0 / D, EPS, ALU.mult, ALU.add).then_inc(y_mean, 1)
                dve.wait_ge(y_rstd, b1)
                for t in range(NT):
                    ins = dve.scalar_tensor_tensor(y_out[:, t, :], y_out[:, t, :], st4[:, 4 + t:5 + t], fw[:, :], ALU.mult, ALU.mult)
                ins.then_inc(y_ready2, 1)
                dve.wait_ge(y_ready2, b1)

        @block.tensor
        def _(pe):
            def split_mm(dst, a_hi, a_lo, b_hi, b_lo, first, last):
                pe.matmul(dst, a_hi, b_hi, start=first, stop=False)
                pe.matmul(dst, a_hi, b_lo, start=False, stop=False)
                return pe.matmul(dst, a_lo, b_hi, start=False, stop=last)

            def gemm(s, n, read, v_hi, v_lo):
                pe.wait_ge(hi_ready[s], n)
                pe.wait_ge(lo_ready[s], n)
                pe.wait_ge(z_read[s], read)
                for k in range(KT):
                    c = slice(k * P, (k + 1) * P)
                    last = split_mm(bank[s][:, :], w_hi[:, s, c], w_lo[:, s, c], v_hi[:, k, :], v_lo[:, k, :], k == 0, k == KT - 1)
                last.then_inc(gemm_done[s], 1)

            pe.wait_ge(const_in, 16 * 6)
            pe.wait_ge(zeroed, 6)
            ident = mk[:, IDENT, :]
            with pe.Fori(0, NB) as b:
                b1 = pe.snap(b + 1)
                u = pe.snap(b * PAIRS + 1)
                v = pe.snap(b * EVACS + 1)
                pe.wait_ge(x_normed, b1)
                for s in range(2):
                    pe.wait_ge(z_read[s], v)
                for k in range(KT):
                    r = k % 2
                    if k >= 2:
                        pe.wait_ge(h32_ready[r], b * (KT // 2) + k // 2)
                    for t in range(NT):
                        ins = pe.transpose(bank[r][:, t * P:(t + 1) * P], x_sb[:, t, k * P:(k + 1) * P], ident)
                    ins.then_inc(xt_done[r], 1)
                for r in range(2):
                    pe.wait_ge(h_lo[r], b1 * (KT // 2))
                    pe.wait_ge(h_hi[r], b1 * (KT // 2))
                gemm(0, u, v, hT_hi, hT_lo)
                gemm(1, u, v, hT_hi, hT_lo)
                gemm(0, u + 1, v + 1, hT_hi, hT_lo)
                pe.wait_ge(hi_ready[1], u + 1)
                pe.wait_ge(lo_ready[1], u + 1)
                pe.wait_ge(z_read[1], v + 1)
                pe.matmul(bank[1][:, :], w_hi[:, 1, 0:P], hT_hi[:, 0, :], start=True, stop=True).then_inc(gemm_done[1], 1)
                for g in range(2):
                    for t in range(NT):
                        c = (g * NT + t) * CH
                        ins = pe.transpose(bank[2 + g][:, t * P:(t + 1) * P], vb[:, c:c + P], ident)
                    ins.then_inc(vwin_t[g], 1)
                pe.wait_ge(z_read[0], v + 2)
                for t in range(NT):
                    ins = pe.transpose(bank[4][:, t * P:(t + 1) * P], ba_t[:, t * P:(t + 1) * P], ident)
                ins.then_inc(ba_done, 1)
                pe.wait_ge(g_ready, b1)
                gs = sc_all[:, G, :, :].rearrange("p t h -> p (t h)")
                for i, m in enumerate((UPTO, ONES, AFTER)):
                    ins = pe.matmul(bank[5][:, i * NT * H:(i + 1) * NT * H], mk[:, m, :], gs, start=True, stop=True)
                ins.then_inc(cums, 1)

                def project(par, n1, u, v):
                    for k in range(HEAD_TILES):
                        gemm(k % 2, u + k // 2, v + k // 2, hT_hi, hT_lo)

                def head(par, n1):
                    n4, n6, n7 = (pe.snap((n1 - 1) * i) for i in (NT, LEVELS, LEVELS + 1))
                    q, k, vv = (qkv[:, par, i, :] for i in range(3))
                    for i, src in enumerate((q, k, vv)):
                        pe.wait_ge(act_q[i], n1)
                        for t in range(NT):
                            ins = pe.transpose(bch(2 + i)[:, t, :], src[:, t * P:(t + 1) * P], ident)
                        ins.then_inc(tr_done[i], 1)
                    pe.wait_ge(gup_ready, n1)
                    pe.matmul(bank[5][:, :], mk[:, AFTER, :], g_up.rearrange("p t c -> p (t c)"), start=True, stop=True
                              ).then_inc(dec_done, 1)
                    for t in range(NT):
                        c = slice(t * P, (t + 1) * P)
                        ins = pe.matmul(bch(6)[:, t, :], k[:, c], k[:, c], start=True, stop=True)
                        ins2 = pe.matmul(bch(7)[:, t, :], k[:, c], q[:, c], start=True, stop=True)
                    ins2.then_inc(qk_done, 1)
                    pe.wait_ge(dec_ready, n1)
                    pe.wait_ge(pt_ready, n6 + 1)
                    for t in range(NT):
                        ins = pe.transpose(bch(5)[:, t, :], pt_sb[0][:, t, :], ident)
                    ins.then_inc(p_done, 1)
                    pe.wait_ge(kd_ready, n1)
                    pe.wait_ge(vr_ready, n1)

                    def accumulate(l):
                        pe.wait_ge(p_ready, n7 + (l + 1))
                        pe.wait_ge(tt_ready, n7 + l)
                        for t in range(NT):
                            ins = pe.matmul(bch(4)[:, t, :], p_sb[l % 2][:, t, :], tt_sb[(l - 1) % 2][:, t, :], start=True, stop=True)
                        ins.then_inc(tt_done, 1)

                    for l in range(1, LEVELS + 1):
                        pe.wait_ge(p_ready, n7 + l)
                        pe.wait_ge(pt_ready, n6 + l)
                        for t in range(NT):
                            ins = pe.matmul(bch(5)[:, t, :], pt_sb[(l - 1) % 2][:, t, :], p_sb[(l - 1) % 2][:, t, :], start=True, stop=True)
                        ins.then_inc(p_done, 1)
                        if l < LEVELS:
                            for t in range(NT):
                                ins = pe.matmul(bch(3)[:, t, :], p_sb[(l - 1) % 2][:, t, :], pt_sb[(l - 1) % 2][:, t, :], start=True, stop=True)
                            ins.then_inc(pt_done, 1)
                        if l > 1:
                            accumulate(l - 1)
                    accumulate(LEVELS)
                    tt = tt_sb[LEVELS % 2]
                    pe.wait_ge(tt_ready, n7 + (LEVELS + 1))
                    for t in range(NT):
                        c = slice(t * P, (t + 1) * P)
                        pe.wait_ge(s_ready if t else s0_ready, n4 + t if t else n1)
                        if t == 0:
                            pe.wait_ge(attn_ready, n1)
                        pe.matmul(bank[6][:, 0:P], k[:, c], s_cur[:, t % 2, :], start=True, stop=True).then_inc(ks_done, 1)
                        if t:
                            pe.wait_ge(o1_ready, n4 + t)
                        pe.matmul(bank[2][:, 0:P], q[:, c], s_cur[:, t % 2, :], start=True, stop=True).then_inc(qs_done, 1)
                        pe.wait_ge(r_ready, n4 + (t + 1))
                        pe.matmul(bank[6][:, 0:P], tt[:, t, :], r_sb[:, :], start=True, stop=True).then_inc(y_done, 1)
                        pe.wait_ge(y_ready, n4 + (t + 1))
                        pe.matmul(bank[3][:, 0:P], kd[:, t, :], y_sb[:, t % 2, :], start=True, stop=True).then_inc(ds_done, 1)
                        if t:
                            pe.wait_ge(o_ready, n4 + t)
                        pe.matmul(bank[7][:, 0:P], attn[:, t, :], y_sb[:, t % 2, :], start=True, stop=True).then_inc(ay_done, 1)
                    for g in range(2):
                        if g:
                            pe.wait_ge(pv_read[0], n1)
                        for t in range(NT):
                            cc = g * NT + t
                            ins = pe.matmul(bch(4)[:, t, :], qbd[:, par, cc, :], kb[:, cc * CH:cc * CH + P], start=True, stop=True)
                        ins.then_inc(lg_done[g], 1)
                        pe.wait_ge(prob_ready[g], n1)
                        pe.wait_ge(vwin_ready, b1 * 2)
                        for t in range(NT):
                            ins = pe.transpose(bch(5)[:, t, :], lg[:, t, :], ident)
                        ins.then_inc(prt_done[g], 1)
                        pe.wait_ge(pts_ready[g], n1)
                        for t in range(NT):
                            ins = pe.matmul(bch(4)[:, t, :], vwin[:, g * NT + t, :], pts[:, t, :], start=True, stop=True)
                        ins.then_inc(pv_done[g], 1)
                    pe.wait_ge(o1_ready, n4 + NT)
                    pe.wait_ge(on_ready, n1)
                    for t in range(NT):
                        ins = pe.transpose(bch(2)[:, t, :], o_sb[:, t, :], ident)
                    ins.then_inc(ot_done, 1)
                    pe.wait_ge(pv_read[1], n1)

                with pe.Fori(0, H // 2) as hp:
                    for par in range(2):
                        n1 = pe.snap(b * H + hp * 2 + (par + 1))
                        uu = pe.snap(b * PAIRS + hp * HEAD_TILES + (PRO_TILES // 2 + par * HEAD_TILES // 2 + 1))
                        vv = pe.snap(b * EVACS + hp * HEAD_TILES + (PRO_TILES // 2 + par * HEAD_TILES // 2 + 1))
                        project(par, n1, uu, vv)
                        head(par, n1)

                with pe.Fori(0, KT) as c:
                    uu = pe.snap(b * PAIRS + c * 2 + ((PRO_TILES + H * HEAD_TILES) // 2 + 1))
                    vv = pe.snap(b * EVACS + c * 2 + ((PRO_TILES + H * HEAD_TILES) // 2 + 1))
                    pe.wait_ge(head_dve_done, b1 * H + 1)
                    gemm(0, uu, vv, hT_hi, hT_lo)
                    gemm(1, uu, vv, oa_hi, oa_lo)
                    gemm(0, uu + 1, vv + 1, hT_hi, hT_lo)
                    gemm(1, uu + 1, vv + 1, ob_hi, ob_lo)

                for s in range(2):
                    pe.wait_ge(z_read[s], b1 * EVACS + 1)
                for n in range(2):
                    for q in range(NT):
                        s = q % 2
                        un = u + (PAIRS - OUT_TILES // 2 + n * 2 + q // 2)
                        pe.wait_ge(hi_ready[s], un)
                        pe.wait_ge(lo_ready[s], un)
                        if n == 0:
                            for k in (2 * q, 2 * q + 1):
                                pe.wait_ge(m_hi[k], b1)
                                pe.wait_ge(m_lo[k], b1)
                        for t in range(NT):
                            for kk in range(2):
                                k = 2 * q + kk
                                c = slice(t * P, (t + 1) * P)
                                wc = slice(kk * TB, (kk + 1) * TB)
                                ins = split_mm(bank[OUT_BANKS[n][t]][:, :], hT_hi[:, k, c], hT_lo[:, k, c],
                                               w_hi[:, s, wc], w_lo[:, s, wc], k == 0, k == KT - 1)
                        ins.then_inc(gemm_done[s], 1)
                pe.wait_ge(res_ready, b1)


OUT_BANKS = ((2, 3, 4, 5), (6, 7, 0, 1))


def relative_buckets():
    nb, dist = 16, 128
    rel = np.arange(2 * CH)[None, :] - CH - np.arange(CH)[:, None]
    n = np.abs(rel)
    exact = nb // 2
    large = exact + (np.log(np.maximum(n, 1) / exact) / np.log(dist / exact) * (nb - exact)).astype(np.int32)
    return ((rel > 0) * nb + np.where(n < exact, n, np.minimum(large, nb - 1))).astype(np.int32)


def kernel(x, norm_w, w_in, conv_w, a_log, dt_bias, gdn_norm_w, attn_sinks, w_o_a, w_o_b, w_out, rel_bias, final_norm_w):
    import concourse.bacc as bacc
    from concourse.bass_utils import run_bass_kernel_spmd

    x, norm_w, w_in, conv_w, a_log, dt_bias, gdn_norm_w, attn_sinks, w_o_a, w_o_b, w_out, rel_bias, final_norm_w = (
        np.asarray(a) for a in (x, norm_w, w_in, conv_w, a_log, dt_bias, gdn_norm_w, attn_sinks, w_o_a, w_o_b, w_out,
                                rel_bias, final_norm_w))
    f32 = np.float32
    w = w_in[0]
    at = np.cumsum([0, D, D, D, H, H, D, D, 2 * DH, 2 * DH, D, D, D])
    (qa, ka, va, b_a, a_a, z_a, qb, kb_, vb_, z_b, g_a, g_b) = (w[:, at[i]:at[i + 1]] for i in range(12))

    def tile(m):
        return m.reshape(KT, P, P).transpose(1, 0, 2).reshape(P, TILE)

    def head(m, h):
        return m[:, h * P:(h + 1) * P]

    pair = np.arange(D).reshape(2, H, DH).transpose(1, 0, 2).reshape(-1)
    qb, z_b, wob = qb[:, pair], z_b[:, pair], w_o_b[0][pair]
    ba_w = np.concatenate([b_a, a_a, np.zeros((D, P - 2 * H), f32)], axis=1)
    tiles = [tile(kb_), tile(vb_), tile(ba_w), np.zeros((P, TILE), f32)]
    for h in range(H):
        tiles += [tile(head(m, h)) for m in (qa, ka, va, z_a, qb, z_b)]
    for c in range(KT):
        tiles += [tile(head(m, c)) for m in (g_a, w_o_a[0], g_b, wob)]
    for n in range(2):
        for q in range(NT):
            m = w_out[0][2 * q * P:(2 * q + 2) * P, n * TB:(n + 1) * TB]
            tiles.append(m.reshape(2, P, TB).transpose(1, 0, 2).reshape(P, TILE))
    w_tiles = np.stack(tiles + tiles[:2])

    conv = conv_w[0].reshape(CONV, 3, H, P).transpose(2, 3, 1, 0).reshape(H, P, 3 * CONV)
    sinks = np.repeat(attn_sinks[0].reshape(2, H).T, CH, axis=1)[:, :, None]
    step_const = np.concatenate([conv, sinks], axis=2)
    full = rel_bias[relative_buckets()].transpose(2, 0, 1)
    full = full.reshape(2, H, CH, P).transpose(1, 0, 2, 3).reshape(H, P, P)
    bias = np.empty((NB, H, P, 2, P), f32)
    bias[:, :, :, 0] = full
    bias[:, :, :, 1] = full
    bias[0, :, :, 0, 0:CH] = NEG
    bias = bias.reshape(NB * H, P, 2, P)

    i = np.arange(P)
    masks = np.stack([np.eye(P), i[:, None] <= i[None, :], i[:, None] > i[None, :], -1.0 * (i[:, None] < i[None, :]),
                      np.ones((P, P))]).astype(f32).transpose(1, 0, 2)
    ins = {
        "x": x[0].reshape(NB, NT, P, D).transpose(0, 2, 1, 3),
        "w_tiles": w_tiles,
        "norm_w": norm_w[0].reshape(KT, P).T,
        "gdn_norm_w": gdn_norm_w[0][:, None],
        "decay_bias": np.broadcast_to(np.stack([a_log[0], dt_bias[0]])[None], (P, 2, H)),
        "step_const": step_const,
        "bias": bias,
        "final_w": np.broadcast_to(final_norm_w[None], (P, D)),
        "masks": masks,
    }
    nc = bacc.Bacc("TRN2", target_bir_lowering=False, num_devices=1, dynamic_dma_scratch_size=1024)
    arrays, args = {}, []
    for name, a in ins.items():
        a = np.ascontiguousarray(a)
        arrays[f"in_{name}"] = a
        args.append(nc.dram_tensor(f"in_{name}", a.shape, mybir.dt.from_np(a.dtype), kind="ExternalInput").ap())
    out = nc.dram_tensor("out_y", (NB, P, NT, D), F32, kind="ExternalOutput").ap()
    build_program(nc, *args, out)
    res = run_bass_kernel_spmd(nc, [arrays], core_ids=[0])
    y = res.results[0]["out_y"]
    return np.ascontiguousarray(y.transpose(0, 2, 1, 3)).reshape(1, SEQ, D)
```

```python
from contextlib import ExitStack

import numpy as np
import concourse.bass as bass
from concourse import mybir

P = 128
D = 1024
KT = D // P
SEQ = 2048
TB = 512
NB = SEQ // TB
NT = TB // P
H = 8
CH = 64
NC = TB // CH
DH = 64
CONV = 4
TILE = KT * P
EPS = 1e-6
NEG = -3.0e38
LEVELS = 6

HEAD_TILES = 6
PRO_TILES = 4
GATE_TILES = 4
OUT_TILES = 8
TILES = PRO_TILES + H * HEAD_TILES + H * GATE_TILES + OUT_TILES
PAIRS = TILES // 2
EVACS = (TILES - OUT_TILES) // 2

F32 = mybir.dt.float32
F32R = mybir.dt.float32r
ALU = mybir.AluOpType
ACT = mybir.ActivationFunctionType
AX = mybir.AxisListType.X

IDENT, UPTO, AFTER, NEGSTRICT, ONES = range(5)
G, BETA, EGC, EGL, ETAIL = range(5)


class Chain:

    def __init__(self, eng, sem, base):
        self.eng, self.sem, self.base, self.k = eng, sem, base, 0

    def inc(self, ins):
        self.k += 1
        ins.then_inc(self.sem, 1)

    def sync(self):
        self.eng.wait_ge(self.sem, self.base + self.k)

    def link(self, ins):
        self.inc(ins)
        self.sync()


def build_program(nc, x, w_tiles, norm_w, gdn_norm_w, decay_bias, step_const, bias, final_w, masks, out):
    with ExitStack() as ctx:
        def sb(name, shape, dt=F32):
            return ctx.enter_context(nc.sbuf_tensor(name, shape, dt))

        def sem(name, n=None):
            if n is None:
                return ctx.enter_context(nc.semaphore(name))
            return [ctx.enter_context(nc.semaphore(f"{name}{i}")) for i in range(n)]

        hT_hi = sb("hT_hi", [P, KT, TB], F32R)
        hT_lo = sb("hT_lo", [P, KT, TB], F32R)
        oa_hi = sb("oa_hi", [P, H, TB], F32R)
        oa_lo = sb("oa_lo", [P, H, TB], F32R)
        ob_hi = sb("ob_hi", [P, H, TB], F32R)
        ob_lo = sb("ob_lo", [P, H, TB], F32R)
        w_raw = sb("w_raw", [P, 2, TILE])
        w_hi = sb("w_hi", [P, 2, TILE], F32R)
        w_lo = sb("w_lo", [P, 2, TILE], F32R)
        area1 = sb("area1", [P, 8 * TB])
        area2 = sb("area2", [P, 15 * TB])
        kb = sb("kb", [P, CH + TB])
        vb = sb("vb", [P, CH + TB])
        vwin = sb("vwin", [P, NC, P])
        zraw = sb("zraw", [P, 3, CONV - 1 + TB])
        hist = sb("hist", [P, H, 3, CONV - 1])
        za = sb("za", [P, 2, TB])
        zb = sb("zb", [P, 2, TB])
        qbd = sb("qbd", [P, 2, NC, P])
        s_all = sb("s_all", [P, H, P])
        s_cur = sb("s_cur", [P, 2, P])
        r_sb = sb("r_sb", [P, P])
        o1_sb = sb("o1_sb", [P, 2, P])
        y_sb = sb("y_sb", [P, 2, P])
        mk = sb("mk", [P, 5, P])
        fw = sb("fw", [P, D])
        bias_sb = sb("bias_sb", [P, 2, 2, P])
        stc = sb("stc", [P, 2, 3 * CONV + 1])
        nw = sb("nw", [P, KT])
        gnw = sb("gnw", [P, 1])
        db = sb("db", [P, 2, H])
        nea = sb("nea", [P, H])
        ba = sb("ba", [P, NT, 2 * H])
        pa = sb("pa", [P, 6, NT, H])
        sc_all = sb("sc_all", [P, 5, NT, H])
        scs = sb("scs", [P, 2, 5, NT])
        half = sb("half", [P, 8])
        st4 = sb("st4", [P, 12])
        spare = sb("spare", [P, 12])
        sty = sb("sty", [P, 12])
        ssq = sb("ssq", [P, 2, NT])
        ssk = sb("ssk", [P, NT])
        rk = sb("rk", [P, NT])
        qo = sb("qo", [P, 2, NT])
        rqo = sb("rqo", [P, 2, NT])
        kn = sb("kn", [P, NT])
        rk2 = sb("rk2", [P, NT])
        bj = sb("bj", [P, NT])
        negc = sb("negc", [P, NT])
        ksc = sb("ksc", [P, NT])
        iq2 = sb("iq2", [P, NT])
        sso = sb("sso", [P, NT])
        fo = sb("fo", [P, NT])
        mx = sb("mx", [P, NT])
        nmx = sb("nmx", [P, NT])
        psum_row = sb("psum_row", [P, NT])
        esink = sb("esink", [P, NT])
        den = sb("den", [P, NT])
        rden = sb("rden", [P, NT])

        x_sb = area1[:, :].rearrange("p (t c) -> p t c", t=NT)
        merged = area1[:, :].rearrange("p (c t) -> p c t", c=KT)
        qkv = area1[:, 0:6 * TB].rearrange("p (r i t) -> p r i t", r=2, i=3)

        def scratch(i, n=1):
            return area2[:, i * TB:(i + n) * TB]

        def chunks(ap):
            return ap.rearrange("p (t c) -> p t c", t=NT)

        g_up = chunks(scratch(0))
        dec = chunks(scratch(1))
        dec_u = chunks(scratch(2))
        dec_n = chunks(scratch(3))
        p_sb = [chunks(scratch(4)), chunks(scratch(5))]
        pt_sb = [chunks(scratch(6)), chunks(scratch(7))]
        tt_sb = [chunks(scratch(8)), chunks(scratch(9))]
        attn = dec
        kd = chunks(scratch(11))
        vr = chunks(scratch(12))
        o_sb = chunks(scratch(13))
        ez = [scratch(10), scratch(14)]
        lg = dec_n
        pts = dec_u
        y_out = area2[:, 0:8 * TB].rearrange("p (t c) -> p t c", t=NT)
        junk2 = area2[:, 8 * TB:10 * TB]
        h32 = [scratch(10), scratch(11)]
        ba_t = scratch(12)
        ga = scratch(0)
        gb = scratch(1)
        ma = scratch(2)
        mb = scratch(3)

        bank = [ctx.enter_context(nc.psum_tensor(f"bank{i}", [P, TB], F32)) for i in range(8)]

        def bch(i):
            return bank[i][:, :].rearrange("p (t c) -> p t c", t=NT)

        const_in = sem("const_in")
        zeroed = sem("zeroed")
        const_ready = sem("const_ready")
        w_landed = sem("w_landed", 2)
        hi_ready = sem("hi_ready", 2)
        lo_ready = sem("lo_ready", 2)
        gemm_done = sem("gemm_done", 2)
        z_read = sem("z_read", 2)
        x_landed = sem("x_landed")
        x_ssq = sem("x_ssq")
        x_mean = sem("x_mean")
        x_rstd = sem("x_rstd")
        x_normed = sem("x_normed")
        xt_done = sem("xt_done", 2)
        h32_ready = sem("h32_ready", 2)
        h_hi = sem("h_hi", 2)
        h_lo = sem("h_lo", 2)
        ba_done = sem("ba_done")
        vwin_t = sem("vwin_t", 2)
        vwin_ready = sem("vwin_ready")
        pre_exp = sem("pre_exp")
        exps = sem("exps")
        sp_in = sem("sp_in")
        lns = sem("lns")
        g_ready = sem("g_ready")
        cums = sem("cums")
        ecums = sem("ecums")
        step_in = sem("step_in")
        conv_ready = sem("conv_ready", 3)
        zraw_free = sem("zraw_free")
        tanh_z = sem("tanh_z", 5)
        silu_ready = sem("silu_ready", 3)
        head_dve_done = sem("head_dve_done")
        sc_ready = sem("sc_ready")
        gup_ready = sem("gup_ready")
        tr_done = sem("tr_done", 3)
        dec_done = sem("dec_done")
        kk_done = sem("kk_done")
        qk_done = sem("qk_done")
        ssq_ready = sem("ssq_ready", 2)
        ssk_ready = sem("ssk_ready")
        rk_ready = sem("rk_ready")
        b_ready = sem("b_ready")
        ksc_ready = sem("ksc_ready")
        kd_ready = sem("kd_ready")
        vr_ready = sem("vr_ready")
        dec_ready = sem("dec_ready")
        decn_ready = sem("decn_ready")
        attn_ready = sem("attn_ready")
        p_done = sem("p_done")
        pt_done = sem("pt_done")
        tt_done = sem("tt_done")
        p_ready = sem("p_ready")
        pt_ready = sem("pt_ready")
        tt_ready = sem("tt_ready")
        s0_ready = sem("s0_ready")
        ks_done = sem("ks_done")
        qs_done = sem("qs_done")
        r_ready = sem("r_ready")
        y_done = sem("y_done")
        y_ready = sem("y_ready")
        ds_done = sem("ds_done")
        ay_done = sem("ay_done")
        s_ready = sem("s_ready")
        o1_ready = sem("o1_ready")
        o_ready = sem("o_ready")
        sso_ready = sem("sso_ready")
        qo_ready = sem("qo_ready")
        rqo_ready = sem("rqo_ready")
        on_ready = sem("on_ready")
        ot_done = sem("ot_done")
        lg_done = sem("lg_done", 2)
        nmx_ready = sem("nmx_ready", 2)
        exp_ready = sem("exp_ready", 2)
        prob_ready = sem("prob_ready", 2)
        prt_done = sem("prt_done", 2)
        pts_ready = sem("pts_ready", 2)
        pv_done = sem("pv_done", 2)
        pv_read = sem("pv_read", 2)
        merged_ready = sem("merged_ready")
        m_hi = sem("m_hi", KT)
        m_lo = sem("m_lo", KT)
        x2_landed = sem("x2_landed")
        res_half = sem("res_half")
        res_ready = sem("res_ready")
        y_ssq = sem("y_ssq")
        y_mean = sem("y_mean")
        y_rstd = sem("y_rstd")
        y_ready2 = sem("y_final")
        y_stored = sem("y_stored")
        dve_init, dve_pro, dve_proj, dve_head = sem("dve_init"), sem("dve_pro"), sem("dve_proj"), sem("dve_head")
        act_pro = sem("act_pro")
        DVE_PRO, DVE_HEAD, DVE_PROJ, ACT_PRO = 12, 21, 10, 3

        block = ctx.enter_context(nc.Block())

        @block.sync
        def _(sp):
            for s in range(2):
                sp.dma_start(w_raw[:, s, :], w_tiles[s]).then_inc(w_landed[s], 16)
            with sp.Fori(0, NB) as b:
                with sp.Fori(0, PAIRS) as u:
                    used = sp.snap(b * PAIRS + u + 1)
                    for s in range(2):
                        sp.wait_ge(hi_ready[s], used)
                        sp.wait_ge(lo_ready[s], used)
                        sp.dma_start(w_raw[:, s, :], w_tiles[bass.ds(u * 2 + (2 + s), 1)].rearrange("o p n -> p (o n)")
                                     ).then_inc(w_landed[s], 16)

        @block.gpsimd
        def _(pool):
            pool.memset(kb[:, :], 0.0).then_inc(zeroed, 1)
            pool.memset(vb[:, :], 0.0).then_inc(zeroed, 1)
            pool.memset(qbd[:, :, :, :], 0.0).then_inc(zeroed, 1)
            pool.memset(s_all[:, :, :], 0.0).then_inc(zeroed, 1)
            pool.memset(hist[:, :, :, :], 0.0).then_inc(zeroed, 1)
            pool.memset(half[:, :], -0.5).then_inc(zeroed, 1)
            for i, s in enumerate((*z_read, zraw_free, head_dve_done, head_dve_done, ot_done, ot_done, merged_ready, y_stored, res_ready)):
                pool.memset(spare[:, i:i + 1], 0.0).then_inc(s, 1)
            pool.wait_ge(zeroed, 6)
            pool.wait_ge(const_in, 16 * 6)

            def low_part(s, n):
                pool.wait_ge(hi_ready[s], n)
                pool.tensor_tensor(w_lo[:, s, :], w_raw[:, s, :], w_hi[:, s, :].bitcast(F32),
                                   ALU.subtract).then_inc(lo_ready[s], 1)

            def power(dst, src, n, src_ready, value, ready):
                pool.wait_ge(src_ready, value)
                pool.tensor_tensor(dst, src, half[:, 0:n], ALU.pow).then_inc(ready, 1)

            for s in range(2):
                low_part(s, 1)
            power(st4[:, 4:8], st4[:, 8:12], NT, x_mean, 1, x_rstd)
            with pool.Fori(0, NB) as b:
                b1 = pool.snap(b + 1)
                ub = pool.snap(b * PAIRS)
                for k in range(PRO_TILES):
                    low_part(k % 2, ub + (k // 2 + 2))
                u0 = pool.snap(b * PAIRS + PRO_TILES // 2)
                for k in range(HEAD_TILES):
                    low_part(k % 2, u0 + (k // 2 + 2))

                def decays(par, n1):
                    pool.wait_ge(sc_ready, n1)
                    pool.tensor_tensor(g_up, mk[:, UPTO:UPTO + 1, :].to_broadcast([P, NT, P]),
                                       scs[:, par, G, :, None].to_broadcast([P, NT, P]), ALU.mult).then_inc(gup_ready, 1)

                pool.wait_ge(y_stored, b * 16 + 1)
                decays(0, pool.snap(b * H + 1))

                def head(par, n1, u):
                    if u is None:
                        tiles = iter(())
                    else:
                        tiles = iter([(k % 2, k // 2 + 2) for k in range(HEAD_TILES)])

                    def low(n):
                        for _ in range(n):
                            for s, i in [next(tiles, (None, None))]:
                                if s is not None:
                                    low_part(s, u + i)

                    power(rk[:, :], ssk[:, :], NT, ssk_ready, n1, rk_ready)
                    pool.wait_ge(dec_ready, n1)
                    pool.tensor_tensor(dec_n, dec, mk[:, NEGSTRICT:NEGSTRICT + 1, :].to_broadcast([P, NT, P]),
                                       ALU.mult).then_inc(decn_ready, 1)
                    low(2)
                    if u is not None:
                        pool.wait_ge(dec_done, n1)
                        decays(1 - par, pool.snap(n1 + 1))
                    low(2)
                    power(rqo[:, :, :].rearrange("p a t -> p (a t)"), qo[:, :, :].rearrange("p a t -> p (a t)"), 2 * NT,
                          qo_ready, n1, rqo_ready)
                    low(2)

                def pair(first, h0, last):
                    for par in range(2):
                        n1 = pool.snap(first + (par + 1))
                        u = None if last and par else pool.snap(
                            b * PAIRS + h0 * (HEAD_TILES // 2) + ((par + 1) * (HEAD_TILES // 2) + PRO_TILES // 2))
                        head(par, n1, u)

                with pool.Fori(0, H // 2 - 1) as hp:
                    pair(b * H + hp * 2, hp * 2, False)
                pair(b * H + (H - 2), H - 2, True)
                with pool.Fori(0, H) as c:
                    u = pool.snap(b * PAIRS + c * (GATE_TILES // 2) + (PRO_TILES + H * HEAD_TILES) // 2)
                    for k in range(GATE_TILES):
                        low_part(k % 2, u + (k // 2 + 2))
                for k in range(OUT_TILES):
                    low_part(k % 2, ub + (PAIRS - OUT_TILES // 2 + k // 2 + 2))
                    if k == 1:
                        power(st4[:, 4:8], st4[:, 8:12], NT, x_mean, b1 + 1, x_rstd)
                power(sty[:, 4:8], sty[:, 8:12], NT, y_mean, b1, y_rstd)

        @block.scalar
        def _(act):
            act.dma_start(mk[:, :, :], masks).then_inc(const_in, 16)
            act.dma_start(fw[:, :], final_w).then_inc(const_in, 16)
            act.dma_start(nw[:, :], norm_w).then_inc(const_in, 16)
            act.dma_start(gnw[:, :], gdn_norm_w).then_inc(const_in, 16)
            act.dma_start(db[:, :, :], decay_bias).then_inc(const_in, 16)
            act.dma_start(bias_sb[:, 0, :, :], bias[0]).then_inc(const_in, 16)

            def high_part(s, n, n16):
                act.wait_ge(w_landed[s], n16)
                act.activation(w_hi[:, s, :], w_raw[:, s, :], ACT.Copy).then_inc(hi_ready[s], 1)

            def product(s, n, n16):
                act.wait_ge(gemm_done[s], n)
                high_part(s, n + 1, n16 + 16)

            for s in range(2):
                high_part(s, 1, 16)
            act.wait_ge(const_in, 16 * 6)
            act.wait_ge(zeroed, 6)
            act.activation(nea[:, :], db[:, 0, :], ACT.Exp).then_inc(const_ready, 1)

            def load_x(j):
                act.dma_start(x_sb, x[bass.ds(j, 1)].rearrange("o p t c -> p (o t) c")).then_inc(x_landed, 16)

            def square_x(j):
                act.wait_ge(x_landed, (j + 1) * 16)
                for t in range(NT):
                    act.activation(junk2, x_sb[:, t, :], ACT.Square, accum_out=st4[:, t:t + 1]).then_inc(x_ssq, 1)
                    act.wait_ge(x_ssq, j * NT + (t + 1))

            def h_high(j, k):
                r = k % 2
                act.wait_ge(h32_ready[r], j * (KT // 2) + (k // 2 + 1))
                act.activation(hT_hi[:, k, :], h32[r], ACT.Copy).then_inc(h_hi[r], 1)

            load_x(0)
            square_x(0)
            for k in range(KT):
                h_high(0, k)
            with act.Fori(0, NB) as b:
                b1 = act.snap(b + 1)
                ub = act.snap(b * PAIRS + 1)
                ub16 = act.snap(b * (PAIRS * 16) + 16)
                ch = Chain(act, act_pro, act.snap(b * ACT_PRO))
                ch.inc(act.activation(kb[:, 0:CH], kb[:, TB:TB + CH], ACT.Copy))
                ch.link(act.activation(vb[:, 0:CH], vb[:, TB:TB + CH], ACT.Copy))
                for k, dst in enumerate((kb, vb)):
                    product(k, ub, ub16)
                    act.activation(dst[:, CH:CH + TB], bank[k][:, :], ACT.Copy).then_inc(z_read[k], 1)
                product(0, ub + 1, ub16 + 16)
                act.activation(ba_t, bank[0][:, :], ACT.Copy).then_inc(z_read[0], 1)
                product(1, ub + 1, ub16 + 16)
                act.activation(st4[:, 0:1], bank[1][:, 0:1], ACT.Copy).then_inc(z_read[1], 1)
                for v in range(2):
                    act.wait_ge(vwin_t[v], b1)
                    act.activation(vwin[:, v * NT:(v + 1) * NT, :], bch(2 + v), ACT.Copy).then_inc(vwin_ready, 1)
                act.wait_ge(pre_exp, b1)
                ch.inc(act.activation(pa[:, 2, :, :], ba[:, :, 0:H], ACT.Exp, scale=-1.0))
                act.activation(pa[:, 3, :, :], pa[:, 1, :, :], ACT.Exp).then_inc(exps, 1)
                act.wait_ge(sp_in, b1)
                act.activation(pa[:, 1, :, :], pa[:, 4, :, :], ACT.Ln).then_inc(lns, 1)
                act.wait_ge(cums, b1)
                act.activation(sc_all[:, EGC:ETAIL + 1, :, :].rearrange("p q t h -> p (q t h)"),
                               bank[5][:, 0:3 * NT * H], ACT.Exp).then_inc(ecums, 1)
                assert ch.k == ACT_PRO

                def project(par, n1, hh, u, u16, v):
                    act.wait_ge(head_dve_done, n1)
                    act.wait_ge(ot_done, n1)
                    act.dma_start(stc[:, par, :], step_const[bass.ds(hh, 1)].rearrange("o p n -> p (o n)")
                                  ).then_inc(step_in, 16)
                    act.dma_start(bias_sb[:, par, :, :], bias[bass.ds(n1 - 1, 1)].rearrange("o p a n -> p (o a) n")
                                  ).then_inc(step_in, 16)

                    def conv_exp(i):
                        act.wait_ge(conv_ready[i], n1)
                        act.activation(ez[i % 2], qkv[:, par, i, :], ACT.Tanh, scale=0.5).then_inc(tanh_z[i], 1)

                    def conv_in(i):
                        product(i % 2, u + i // 2, u16 + (i // 2) * 16)
                        act.activation(zraw[:, i, CONV - 1:], bank[i % 2][:, :], ACT.Copy).then_inc(z_read[i % 2], 1)

                    act.wait_ge(zraw_free, n1)
                    conv_in(0)
                    yield
                    act.wait_ge(z_read[1], v)
                    conv_exp(0)
                    yield
                    conv_in(1)
                    yield
                    conv_in(2)
                    yield
                    act.wait_ge(z_read[0], v)
                    conv_exp(1)
                    yield
                    product(1, u + 1, u16 + 16)
                    zq = bank[1][:, :].rearrange("p (c t) -> p c t", c=NC)
                    act.activation(qbd[0:DH, par, :, 0:CH], zq[0:DH], ACT.Copy, scale=DH ** -0.5)
                    act.activation(qbd[DH:P, par, :, CH:P], zq[DH:P], ACT.Copy, scale=DH ** -0.5).then_inc(z_read[1], 1)
                    yield
                    act.wait_ge(silu_ready[0], n1)
                    conv_exp(2)
                    yield
                    for i in (3, 4):
                        slot = (i + 1) % 2
                        product(slot, u + 2, u16 + 32)
                        act.wait_ge(silu_ready[i - 2], n1)
                        act.activation(ez[i % 2], bank[slot][:, :], ACT.Tanh, scale=0.5).then_inc(tanh_z[i], 1)
                        yield

                def head(par, n1, fill):
                    n4, n5, n7 = (act.snap((n1 - 1) * i) for i in (NT, LEVELS - 1, LEVELS + 1))

                    sc = scs[:, par, :, :]

                    def squares(dst, src, ready, i, junk):
                        act.wait_ge(tr_done[i], n1)
                        for t in range(NT):
                            ins = act.activation(junk[:, t, :], src[:, t, :], ACT.Square,
                                                 accum_out=dst[:, t:t + 1])
                        ins.then_inc(ready, 1)

                    def scaled(dst, src, scale, ready):
                        for t in range(NT):
                            ins = act.activation(dst[:, t, :], src[:, t, :], ACT.Copy, scale=scale[:, t:t + 1])
                        ins.then_inc(ready, 1)

                    def p_copy(l):
                        act.wait_ge(p_done, n7 + (l + 1))
                        act.activation(p_sb[l % 2], bch(5), ACT.Copy).then_inc(p_ready, 1)

                    def pt_copy(l):
                        act.wait_ge(pt_done, n5 + l)
                        if l == 2:
                            act.wait_ge(tt_ready, n7 + 1)
                        act.activation(pt_sb[l % 2], bch(6), ACT.Copy).then_inc(pt_ready, 1)

                    squares(ssq[:, 1, :], bch(3), ssq_ready[1], 1, tt_sb[1])
                    act.wait_ge(dec_done, n1)
                    act.activation(dec, bch(5), ACT.Exp).then_inc(dec_ready, 1)
                    squares(ssq[:, 0, :], bch(2), ssq_ready[0], 0, p_sb[1])
                    act.wait_ge(ssq_ready[1], n1)
                    fill(1)
                    p_copy(0)
                    act.wait_ge(ksc_ready, n1)
                    scaled(kd, bch(3), ksc, kd_ready)
                    act.wait_ge(ssq_ready[0], n1)
                    p_copy(1)
                    pt_copy(1)
                    act.wait_ge(tr_done[2], n1)
                    scaled(vr, bch(4), kn, vr_ready)
                    p_copy(2)
                    pt_copy(2)
                    sink = stc[:, par, 3 * CONV:3 * CONV + 1]

                    def softmax_exp(g):
                        act.wait_ge(nmx_ready[g], n1)
                        for t in range(NT):
                            act.activation(lg[:, t, :], lg[:, t, :], ACT.Exp, bias=nmx[:, t:t + 1],
                                           accum_out=psum_row[:, t:t + 1])
                        act.activation(esink[:, :], nmx[:, :], ACT.Exp, bias=sink).then_inc(exp_ready[g], 1)

                    def probs_copy(g):
                        act.wait_ge(prt_done[g], n1)
                        act.activation(pts, bch(4), ACT.Copy).then_inc(pts_ready[g], 1)

                    p_copy(3)
                    pt_copy(3)
                    softmax_exp(0)
                    p_copy(4)
                    pt_copy(4)
                    p_copy(5)
                    pt_copy(5)
                    probs_copy(0)
                    fill(1)
                    p_copy(6)
                    fill(1)

                    def state(t):
                        act.wait_ge(qs_done, n4 + (t + 1))
                        act.activation(o1_sb[:, t % 2, :], bank[2][:, 0:P], ACT.Copy, scale=sc[:, EGC, t:t + 1]
                                       ).then_inc(o1_ready, 1)
                        act.wait_ge(y_done, n4 + (t + 1))
                        act.activation(y_sb[:, t % 2, :], bank[5][:, 0:P], ACT.Copy).then_inc(y_ready, 1)

                    def square_o(t):
                        act.wait_ge(o_ready, n4 + (t + 1))
                        ins = act.activation(tt_sb[1][:, t, :], o_sb[:, t, :], ACT.Square, accum_out=sso[:, t:t + 1])
                        if t == NT - 1:
                            ins.then_inc(sso_ready, 1)

                    state(0)
                    softmax_exp(1)
                    state(1)
                    square_o(0)
                    probs_copy(1)
                    fill(1)
                    state(2)
                    square_o(1)
                    fill(1)
                    state(3)
                    square_o(2)
                    square_o(3)
                    fill(9)

                def prepare(par, n1, hh):
                    u = act.snap(b * PAIRS + hh * (HEAD_TILES // 2) + (PRO_TILES // 2 + 1))
                    v = act.snap(b * EVACS + hh * (HEAD_TILES // 2) + (PRO_TILES // 2 + 1))
                    return project(par, n1, hh, u, act.snap(u * 16), v)

                def pair(first, h0, last):
                    for par in range(2):
                        n1 = act.snap(first + (par + 1))
                        gen = iter(()) if last and par else prepare(1 - par, act.snap(n1 + 1), act.snap(h0 + (par + 1)))

                        def fill(n):
                            for _ in range(n):
                                next(gen, None)
                        head(par, n1, fill)

                for _ in prepare(0, act.snap(b * H + 1), 0):
                    pass
                with act.Fori(0, H // 2 - 1) as hp:
                    pair(b * H + hp * 2, hp * 2, False)
                pair(b * H + (H - 2), H - 2, True)

                with act.Fori(0, KT) as c:
                    u = act.snap(b * PAIRS + c * 2 + ((PRO_TILES + H * HEAD_TILES) // 2 + 1))
                    u16 = act.snap(u * 16)
                    v = act.snap(b * EVACS + c * 2 + ((PRO_TILES + H * HEAD_TILES) // 2 + 1))
                    product(0, u, u16)
                    act.wait_ge(z_read[1], v)
                    act.activation(ga, bank[0][:, :], ACT.Tanh, scale=0.5).then_inc(z_read[0], 1)
                    product(1, u, u16)
                    product(0, u + 1, u16 + 16)
                    act.activation(gb, bank[0][:, :], ACT.Tanh, scale=0.5).then_inc(z_read[0], 1)
                    product(1, u + 1, u16 + 16)

                act.wait_ge(merged_ready, b1 * KT + 1)
                act.dma_start(y_out, x[bass.ds(b, 1)].rearrange("o p t c -> p (o t) c")).then_inc(x2_landed, 16)
                for k in range(KT):
                    act.activation(oa_hi[:, k, :], merged[:, k, :], ACT.Copy, scale=0.5).then_inc(m_hi[k], 1)
                act.wait_ge(m_hi[KT - 1], b1)
                for k in range(KT):
                    act.wait_ge(m_lo[k], b1)
                load_x(b1)
                for k in range(OUT_TILES):
                    product(k % 2, ub + (PAIRS - OUT_TILES // 2 + k // 2), ub16 + (PAIRS - OUT_TILES // 2 + k // 2) * 16)
                    if k == 1:
                        square_x(b1)
                    elif 3 <= k < OUT_TILES - 1:
                        h_high(b1, 2 * k - 6)
                        h_high(b1, 2 * k - 5)
                act.wait_ge(res_ready, b1 + 1)
                for t in range(NT):
                    act.activation(junk2, y_out[:, t, :], ACT.Square, accum_out=sty[:, t:t + 1]).then_inc(y_ssq, 1)
                    act.wait_ge(y_ssq, b * NT + (t + 1))
                act.wait_ge(y_ready2, b1)
                act.dma_start(out[bass.ds(b, 1)].rearrange("o p t c -> p (o t) c"), y_out).then_inc(y_stored, 16)
            act.wait_ge(y_stored, NB * 16 + 1)

        @block.vector
        def _(dve):
            dve.wait_ge(const_in, 16 * 6)
            dve.wait_ge(zeroed, 6)
            dve.wait_ge(const_ready, 1)

            def copy(dst, src):
                return dve.tensor_scalar(dst, src, 1.0, None, ALU.mult)

            dve.tensor_scalar(nea[:, :], nea[:, :], -1.0, None, ALU.mult).then_inc(dve_init, 1)
            dve.wait_ge(dve_init, 1)

            def norm_x(j):
                dve.wait_ge(x_ssq, (j + 1) * NT)
                dve.tensor_scalar(st4[:, 8:12], st4[:, 0:4], 1.0 / D, EPS, ALU.mult, ALU.add).then_inc(x_mean, 1)
                dve.wait_ge(x_rstd, j + 1)
                for t in range(NT):
                    ins = dve.tensor_scalar(x_sb[:, t, :], x_sb[:, t, :], st4[:, 4 + t:5 + t], None, ALU.mult)
                ins.then_inc(x_normed, 1)

            def h_parts(j, k):
                r = k % 2
                kk = j * (KT // 2) + (k // 2 + 1)
                dve.wait_ge(xt_done[r], kk)
                if k >= 2:
                    dve.wait_ge(h_lo[r], kk - 1)
                dve.tensor_scalar(h32[r], bank[r][:, :], nw[:, k:k + 1], None, ALU.mult).then_inc(h32_ready[r], 1)
                dve.wait_ge(h_hi[r], kk)
                dve.tensor_tensor(hT_lo[:, k, :], h32[r], hT_hi[:, k, :].bitcast(F32), ALU.subtract).then_inc(h_lo[r], 1)

            norm_x(0)
            for k in range(KT):
                h_parts(0, k)
            with dve.Fori(0, NB) as b:
                b1 = dve.snap(b + 1)
                ch = Chain(dve, dve_pro, dve.snap(b * DVE_PRO))
                dve.wait_ge(ba_done, b1)
                ch.inc(dve.tensor_copy(ba[:, :, :], bch(4)[:, :, 0:2 * H]))
                ch.sync()
                y = pa[:, 0, :, :]
                ch.link(dve.tensor_tensor(y, ba[:, :, H:2 * H], db[:, 1:2, :].to_broadcast([P, NT, H]), ALU.add))
                ch.link(dve.tensor_scalar(pa[:, 1, :, :], y, -1.0, None, ALU.mult))
                dve.tensor_tensor(pa[:, 1, :, :], pa[:, 1, :, :], y, ALU.min).then_inc(pre_exp, 1)
                dve.wait_ge(exps, b1)
                e, w = pa[:, 3, :, :], pa[:, 4, :, :]
                dve.tensor_scalar(w, e, 1.0, None, ALU.add).then_inc(sp_in, 1)
                dve.wait_ge(sp_in, b1)
                ch.link(dve.tensor_scalar(pa[:, 5, :, :], w, -1.0, None, ALU.add))
                ch.link(dve.tensor_tensor(e, e, pa[:, 5, :, :], ALU.subtract))
                ch.link(dve.reciprocal(pa[:, 5, :, :], w))
                ch.link(dve.tensor_tensor(e, e, pa[:, 5, :, :], ALU.mult))
                ch.link(dve.tensor_scalar(y, y, 0.0, None, ALU.max))
                ch.link(dve.tensor_tensor(y, y, e, ALU.add))
                ch.link(dve.tensor_scalar(pa[:, 2, :, :], pa[:, 2, :, :], 1.0, None, ALU.add))
                ch.link(dve.reciprocal(sc_all[:, BETA, :, :], pa[:, 2, :, :]))
                dve.wait_ge(lns, b1)
                ch.link(dve.tensor_tensor(y, y, pa[:, 1, :, :], ALU.add))
                dve.tensor_tensor(sc_all[:, G, :, :], y, nea[:, None, :].to_broadcast([P, NT, H]), ALU.mult).then_inc(g_ready, 1)
                assert ch.k == DVE_PRO, ch.k

                def project(par, n1, hh, v):
                    ch = Chain(dve, dve_proj, dve.snap((n1 - 1) * DVE_PROJ))

                    def silu(i, z, dst, ready):
                        dve.wait_ge(tanh_z[i], n1)
                        dve.scalar_tensor_tensor(dst, ez[i % 2], 1.0, z, ALU.add, ALU.mult).then_inc(ready, 1)
                        yield

                    dve.wait_ge(head_dve_done, n1)
                    dve.wait_ge(ot_done, n1)
                    dve.wait_ge(ecums, b1)
                    copy(scs[:, par, :, :], sc_all[:, :, :, bass.ds(hh, 1)].rearrange("p q t o -> p q (t o)")
                         ).then_inc(sc_ready, 1)
                    ch.inc(copy(zraw[:, :, 0:CONV - 1], hist[:, bass.ds(hh, 1), :, :].rearrange("p o i n -> p (o i) n")))
                    dve.wait_ge(step_in, n1 * 32)
                    for i in range(3):
                        dve.wait_ge(z_read[i % 2], v + i // 2)
                        ch.sync()
                        acc = qkv[:, par, i, :]
                        ch.inc(dve.tensor_scalar(acc, zraw[:, i, 0:TB], stc[:, par, CONV * i:CONV * i + 1], None, ALU.mult))
                        yield
                        for k in range(1, CONV):
                            ch.sync()
                            ins = dve.scalar_tensor_tensor(acc, zraw[:, i, k:k + TB], stc[:, par, CONV * i + k:CONV * i + k + 1],
                                                           acc, ALU.mult, ALU.add)
                            if k < CONV - 1:
                                ch.inc(ins)
                                yield
                            else:
                                ins.then_inc(conv_ready[i], 1)
                        if i == 2:
                            copy(hist[:, bass.ds(hh, 1), :, :].rearrange("p o i n -> p (o i) n"), zraw[:, :, TB:TB + CONV - 1]
                                 ).then_inc(zraw_free, 1)
                            dve.wait_ge(zraw_free, n1 + 1)
                        yield
                        yield from silu(i, acc, acc, silu_ready[i])
                    for i, dst in ((3, za), (4, zb)):
                        slot = (i + 1) % 2
                        yield from silu(i, bank[slot][:, :], dst[:, par, :], z_read[slot])
                    assert ch.k == DVE_PROJ, ch.k

                def head(par, n1, hh, fill):
                    n4, n6, n7 = (dve.snap((n1 - 1) * i) for i in (NT, LEVELS, LEVELS + 1))
                    ch = Chain(dve, dve_head, dve.snap((n1 - 1) * DVE_HEAD))
                    vz = dve.snap(b * EVACS + hh * (HEAD_TILES // 2) + (PRO_TILES // 2 + HEAD_TILES // 2 + 1))
                    sc = scs[:, par, :, :]
                    copy(s_cur[:, 0, :], s_all[:, bass.ds(hh, 1), :].rearrange("p o c -> p (o c)")).then_inc(s0_ready, 1)
                    dve.wait_ge(sc_ready, n1)
                    dve.tensor_scalar(negc[:, :], sc[:, EGC, :], -1.0, None, ALU.mult)
                    dve.wait_ge(ssq_ready[1], n1)
                    dve.tensor_scalar(ssk[:, :], ssq[:, 1, :], 4 * EPS, None, ALU.add).then_inc(ssk_ready, 1)
                    dve.wait_ge(dec_ready, n1)
                    ch.inc(dve.tensor_tensor(dec_u, dec, mk[:, UPTO:UPTO + 1, :].to_broadcast([P, NT, P]), ALU.mult))
                    dve.wait_ge(rk_ready, n1)
                    dve.wait_ge(ssk_ready, n1)
                    ch.inc(dve.scalar_tensor_tensor(kn[:, :], rk[:, :], 0.5, ssk[:, :], ALU.mult, ALU.mult))
                    ch.link(dve.tensor_tensor(rk2[:, :], rk[:, :], rk[:, :], ALU.mult))
                    dve.tensor_tensor(bj[:, :], rk2[:, :], sc[:, BETA, :], ALU.mult).then_inc(b_ready, 1)
                    dve.wait_ge(b_ready, n1)
                    dve.tensor_tensor(ksc[:, :], bj[:, :], sc[:, ETAIL, :], ALU.mult).then_inc(ksc_ready, 1)
                    dve.wait_ge(kk_done, n1)
                    dve.wait_ge(decn_ready, n1)
                    for t in range(NT):
                        ins = dve.scalar_tensor_tensor(pt_sb[0][:, t, :], bch(6)[:, t, :], bj[:, t:t + 1], dec_n[:, t, :],
                                                       ALU.mult, ALU.mult)
                    ins.then_inc(pt_ready, 1)
                    dve.wait_ge(pt_ready, n6 + 1)
                    dve.tensor_tensor(tt_sb[0], pt_sb[0], mk[:, IDENT:IDENT + 1, :].to_broadcast([P, NT, P]), ALU.add
                                      ).then_inc(tt_ready, 1)
                    dve.wait_ge(qk_done, n1)
                    for t in range(NT):
                        ins = dve.scalar_tensor_tensor(attn[:, t, :], bch(7)[:, t, :], bj[:, t:t + 1], dec_u[:, t, :],
                                                       ALU.mult, ALU.mult)
                    ins.then_inc(attn_ready, 1)
                    dve.wait_ge(ssq_ready[0], n1)
                    ch.link(dve.tensor_scalar(qo[:, 0, :], ssq[:, 0, :], 4 * EPS, None, ALU.add))
                    ch.inc(dve.reciprocal(iq2[:, :], qo[:, 0, :]))

                    def add_tt(l):
                        dve.wait_ge(tt_ready, n7 + l)
                        dve.wait_ge(tt_done, n6 + l)
                        dve.tensor_tensor(tt_sb[l % 2], bch(7), tt_sb[(l - 1) % 2], ALU.add).then_inc(tt_ready, 1)

                    sink = stc[:, par, 3 * CONV:3 * CONV + 1]

                    def logits(g):
                        dve.wait_ge(lg_done[g], n1)
                        if g:
                            dve.wait_ge(prt_done[0], n1)
                            ch.inc(dve.tensor_tensor(lg, bch(3), bias_sb[:, par, 1:2, :].to_broadcast([P, NT, P]), ALU.add))
                        else:
                            dve.wait_ge(attn_ready, n1)
                            ch.inc(dve.tensor_tensor(lg[:, 0, :], bank[3][:, 0:P], bias_sb[:, par, 0, :], ALU.add))
                            ch.inc(dve.tensor_tensor(lg[:, 1:NT, :], bch(3)[:, 1:NT, :],
                                                     bias_sb[:, par, 1:2, :].to_broadcast([P, NT - 1, P]), ALU.add))
                        ch.sync()
                        ch.link(dve.tensor_reduce(mx[:, :], lg, AX, ALU.max))
                        dve.tensor_scalar(nmx[:, :], mx[:, :], sink, -1.0, ALU.max, ALU.mult).then_inc(nmx_ready[g], 1)

                    def quotient(g):
                        dve.wait_ge(exp_ready[g], n1)
                        ch.link(dve.tensor_tensor(den[:, :], psum_row[:, :], esink[:, :], ALU.add))
                        ch.link(dve.reciprocal(rden[:, :], den[:, :]))
                        dve.tensor_tensor(lg, lg, rden[:, :, None].to_broadcast([P, NT, P]), ALU.mult).then_inc(prob_ready[g], 1)

                    def gated(g):
                        dve.wait_ge(z_read[1], vz)
                        dve.wait_ge(pv_done[g], n1)
                        part = slice(g * NT * CH, (g + 1) * NT * CH)
                        for lo, hi in ((0, CH), (CH, P)):
                            zg = zb[lo:hi, par, part].rearrange("p (u t) -> p u t", u=NT)
                            ins = dve.tensor_tensor(zg, bch(3)[lo:hi, :, lo:hi], zg, ALU.mult)
                        ins.then_inc(pv_read[g], 1)

                    fill(2)
                    add_tt(1)
                    logits(0)
                    add_tt(2)
                    fill(1)
                    add_tt(3)
                    quotient(0)
                    fill(1)
                    add_tt(4)
                    add_tt(5)
                    gated(0)
                    fill(1)
                    add_tt(6)
                    dve.wait_ge(vr_ready, n1)
                    for t in range(NT):
                        dve.wait_ge(ks_done, n4 + (t + 1))
                        dve.scalar_tensor_tensor(r_sb[:, :], bank[5][:, 0:P], negc[:, t:t + 1], vr[:, t, :], ALU.mult, ALU.add
                                                 ).then_inc(r_ready, 1)
                        if t == 0:
                            logits(1)
                        else:
                            fill(1)
                        dve.wait_ge(s_ready if t else s0_ready, n4 + t if t else n1)
                        dve.wait_ge(ds_done, n4 + (t + 1))
                        dve.scalar_tensor_tensor(s_cur[:, (t + 1) % 2, :], s_cur[:, t % 2, :], sc[:, EGL, t:t + 1], bank[6][:, 0:P],
                                                 ALU.mult, ALU.add).then_inc(s_ready, 1)
                        dve.wait_ge(ay_done, n4 + (t + 1))
                        dve.wait_ge(o1_ready, n4 + (t + 1))
                        dve.tensor_tensor(o_sb[:, t, :], bank[7][:, 0:P], o1_sb[:, t % 2, :], ALU.add).then_inc(o_ready, 1)
                        if t == 0:
                            quotient(1)
                        elif t == 1:
                            gated(1)
                            dve.wait_ge(pv_read[1], n1)
                            obh = ob_hi[:, bass.ds(hh, 1), :].rearrange("p o t -> p (o t)")
                            ch.inc(dve.tensor_scalar(obh, zb[:, par, :], 0.5, None, ALU.mult))
                        elif t == 2:
                            ch.sync()
                            ch.inc(dve.scalar_tensor_tensor(ob_lo[:, bass.ds(hh, 1), :].rearrange("p o t -> p (o t)"), zb[:, par, :], 0.5,
                                                            obh.bitcast(F32), ALU.mult, ALU.subtract))
                        if t < NT - 1:
                            fill(1 if t else 2)
                    dve.wait_ge(s_ready, n4 + NT)
                    ch.inc(copy(s_all[:, bass.ds(hh, 1), :].rearrange("p o c -> p (o c)"), s_cur[:, 0, :]))
                    dve.wait_ge(sso_ready, n1)
                    ch.link(dve.tensor_tensor(qo[:, 1, :], sso[:, :], iq2[:, :], ALU.mult))
                    dve.tensor_scalar(qo[:, 1, :], qo[:, 1, :], 1.0 / (P * P), EPS, ALU.mult, ALU.add).then_inc(qo_ready, 1)
                    fill(2)
                    dve.wait_ge(rqo_ready, n1)
                    ch.link(dve.scalar_tensor_tensor(fo[:, :], rqo[:, 0, :], 0.5 * float(P) ** -0.5, rqo[:, 1, :], ALU.mult, ALU.mult))
                    dve.tensor_tensor(o_sb, o_sb, fo[:, :, None].to_broadcast([P, NT, P]), ALU.mult).then_inc(on_ready, 1)
                    fill(1)
                    dve.wait_ge(ot_done, n1 + 2)
                    dve.wait_ge(z_read[0], vz)
                    zat = za[:, par, :]
                    ch.link(dve.scalar_tensor_tensor(zat, bank[4][:, :], gnw[:, 0:1], zat, ALU.mult, ALU.mult))
                    oah = oa_hi[:, bass.ds(hh, 1), :].rearrange("p o t -> p (o t)")
                    ch.link(dve.tensor_scalar(oah, zat, 1.0, None, ALU.mult))
                    dve.tensor_tensor(oa_lo[:, bass.ds(hh, 1), :].rearrange("p o t -> p (o t)"), zat, oah.bitcast(F32), ALU.subtract
                                      ).then_inc(head_dve_done, 1)
                    fill(99)
                    assert ch.k == DVE_HEAD, ch.k

                def prepare(par, n1, hh):
                    v = dve.snap(b * EVACS + hh * (HEAD_TILES // 2) + (PRO_TILES // 2 + 2))
                    return project(par, n1, hh, v)

                def pair(first, h0, last):
                    for par in range(2):
                        n1 = dve.snap(first + (par + 1))
                        gen = iter(()) if last and par else prepare(1 - par, dve.snap(n1 + 1), dve.snap(h0 + (par + 1)))

                        def fill(n):
                            for _ in range(n):
                                next(gen, None)
                        head(par, n1, dve.snap(h0 + par), fill)

                for _ in prepare(0, dve.snap(b * H + 1), 0):
                    pass
                with dve.Fori(0, H // 2 - 1) as hp:
                    pair(b * H + hp * 2, hp * 2, False)
                pair(b * H + (H - 2), H - 2, True)

                with dve.Fori(0, KT) as c:
                    v = dve.snap(b * EVACS + c * 2 + ((PRO_TILES + H * HEAD_TILES) // 2 + 2))
                    u = dve.snap(b * PAIRS + c * 2 + ((PRO_TILES + H * HEAD_TILES) // 2 + 1))
                    dve.wait_ge(z_read[0], v)
                    dve.wait_ge(merged_ready, b * KT + c + 1)
                    dve.wait_ge(gemm_done[1], u)
                    dve.scalar_tensor_tensor(ma, ga, 1.0, bank[1][:, :], ALU.add, ALU.mult).then_inc(z_read[1], 1)
                    dve.wait_ge(z_read[1], v)
                    dve.wait_ge(z_read[0], v + 1)
                    dve.wait_ge(gemm_done[1], u + 1)
                    dve.scalar_tensor_tensor(mb, gb, 1.0, bank[1][:, :], ALU.add, ALU.mult).then_inc(z_read[1], 1)
                    dve.wait_ge(z_read[1], v + 1)
                    dve.tensor_tensor(merged[:, bass.ds(c, 1), :].rearrange("p o t -> p (o t)"), ma, mb, ALU.add).then_inc(merged_ready, 1)

                for k in range(KT):
                    dve.wait_ge(m_hi[k], b1)
                    dve.scalar_tensor_tensor(oa_lo[:, k, :], merged[:, k, :], 0.5, oa_hi[:, k, :].bitcast(F32), ALU.mult, ALU.subtract
                                             ).then_inc(m_lo[k], 1)
                norm_x(b1)
                dve.wait_ge(x2_landed, b1 * 16)
                for n in range(2):
                    if n:
                        for k in range(KT):
                            h_parts(b1, k)
                    for s in range(2):
                        dve.wait_ge(gemm_done[s], b1 * PAIRS + (n - 1) * 2)
                    for t in range(NT):
                        half_row = y_out[:, t, n * TB:(n + 1) * TB]
                        ins = dve.tensor_tensor(half_row, bank[OUT_BANKS[n][t]][:, :], half_row, ALU.add)
                    ins.then_inc(res_ready if n else res_half, 1)
                dve.wait_ge(y_ssq, b1 * NT)
                dve.tensor_scalar(sty[:, 8:12], sty[:, 0:4], 1.0 / D, EPS, ALU.mult, ALU.add).then_inc(y_mean, 1)
                dve.wait_ge(y_rstd, b1)
                for t in range(NT):
                    ins = dve.scalar_tensor_tensor(y_out[:, t, :], y_out[:, t, :], sty[:, 4 + t:5 + t], fw[:, :], ALU.mult, ALU.mult)
                ins.then_inc(y_ready2, 1)
                dve.wait_ge(y_ready2, b1)

        @block.tensor
        def _(pe):
            def split_mm(dst, a_hi, a_lo, b_hi, b_lo, first, last):
                pe.matmul(dst, a_hi, b_hi, start=first, stop=False)
                pe.matmul(dst, a_hi, b_lo, start=False, stop=False)
                return pe.matmul(dst, a_lo, b_hi, start=False, stop=last)

            def gemm_steps(s, n, read, v_hi, v_lo):
                pe.wait_ge(hi_ready[s], n)
                pe.wait_ge(lo_ready[s], n)
                pe.wait_ge(z_read[s], read)
                for k in range(KT):
                    c = slice(k * P, (k + 1) * P)
                    last = split_mm(bank[s][:, :], w_hi[:, s, c], w_lo[:, s, c], v_hi[:, k, :], v_lo[:, k, :], k == 0, k == KT - 1)
                    if k == KT - 1:
                        last.then_inc(gemm_done[s], 1)
                    yield

            def gemm(s, n, read, v_hi, v_lo):
                for _ in gemm_steps(s, n, read, v_hi, v_lo):
                    pass

            pe.wait_ge(const_in, 16 * 6)
            pe.wait_ge(zeroed, 6)
            ident = mk[:, IDENT, :]

            def transpose_x(j, k):
                r = k % 2
                if k >= 2:
                    pe.wait_ge(h32_ready[r], j * (KT // 2) + k // 2)
                for t in range(NT):
                    ins = pe.transpose(bank[r][:, t * P:(t + 1) * P], x_sb[:, t, k * P:(k + 1) * P], ident)
                ins.then_inc(xt_done[r], 1)

            pe.wait_ge(x_normed, 1)
            for k in range(KT):
                transpose_x(0, k)
            with pe.Fori(0, NB) as b:
                b1 = pe.snap(b + 1)
                u = pe.snap(b * PAIRS + 1)
                v = pe.snap(b * EVACS + 1)
                for r in range(2):
                    pe.wait_ge(h_lo[r], b1 * (KT // 2))
                    pe.wait_ge(h_hi[r], b1 * (KT // 2))
                gemm(0, u, v, hT_hi, hT_lo)
                gemm(1, u, v, hT_hi, hT_lo)
                gemm(0, u + 1, v + 1, hT_hi, hT_lo)
                pe.wait_ge(hi_ready[1], u + 1)
                pe.wait_ge(lo_ready[1], u + 1)
                pe.wait_ge(z_read[1], v + 1)
                pe.matmul(bank[1][:, :], w_hi[:, 1, 0:P], hT_hi[:, 0, :], start=True, stop=True).then_inc(gemm_done[1], 1)
                pe.wait_ge(res_ready, b1)
                for g in range(2):
                    for t in range(NT):
                        c = (g * NT + t) * CH
                        ins = pe.transpose(bank[2 + g][:, t * P:(t + 1) * P], vb[:, c:c + P], ident)
                    ins.then_inc(vwin_t[g], 1)
                pe.wait_ge(z_read[0], v + 2)
                for t in range(NT):
                    ins = pe.transpose(bank[4][:, t * P:(t + 1) * P], ba_t[:, t * P:(t + 1) * P], ident)
                ins.then_inc(ba_done, 1)

                def sum_decays():
                    pe.wait_ge(g_ready, b1)
                    gs = sc_all[:, G, :, :].rearrange("p t h -> p (t h)")
                    for i, m in enumerate((UPTO, ONES, AFTER)):
                        ins = pe.matmul(bank[5][:, i * NT * H:(i + 1) * NT * H], mk[:, m, :], gs, start=True, stop=True)
                    ins.then_inc(cums, 1)

                def project(u, v):
                    for k in range(HEAD_TILES):
                        yield from gemm_steps(k % 2, u + k // 2, v + k // 2, hT_hi, hT_lo)

                def head(par, n1, fill):
                    n4, n6, n7 = (pe.snap((n1 - 1) * i) for i in (NT, LEVELS, LEVELS + 1))
                    q, k, vv = (qkv[:, par, i, :] for i in range(3))

                    def transposes(i, src):
                        pe.wait_ge(silu_ready[i], n1)
                        for t in range(NT):
                            ins = pe.transpose(bch(2 + i)[:, t, :], src[:, t * P:(t + 1) * P], ident)
                        ins.then_inc(tr_done[i], 1)

                    pe.wait_ge(gup_ready, n1)
                    pe.matmul(bank[5][:, :], mk[:, AFTER, :], g_up.rearrange("p t c -> p (t c)"), start=True, stop=True
                              ).then_inc(dec_done, 1)
                    transposes(1, k)
                    transposes(0, q)
                    for dst, src, done in ((bch(6), k, kk_done), (bch(7), q, qk_done)):
                        for t in range(NT):
                            c = slice(t * P, (t + 1) * P)
                            ins = pe.matmul(dst[:, t, :], k[:, c], src[:, c], start=True, stop=True)
                        ins.then_inc(done, 1)
                    pe.wait_ge(head_dve_done, n1 + 1)
                    transposes(2, vv)
                    fill(9)

                    def square(l):
                        pe.wait_ge(p_ready, n7 + l)
                        pe.wait_ge(pt_ready, n6 + l)
                        for t in range(NT):
                            ins = pe.matmul(bch(5)[:, t, :], pt_sb[(l - 1) % 2][:, t, :], p_sb[(l - 1) % 2][:, t, :], start=True, stop=True)
                        ins.then_inc(p_done, 1)
                        if l < LEVELS:
                            for t in range(NT):
                                ins = pe.matmul(bch(6)[:, t, :], p_sb[(l - 1) % 2][:, t, :], pt_sb[(l - 1) % 2][:, t, :], start=True, stop=True)
                            ins.then_inc(pt_done, 1)

                    def accumulate(l):
                        pe.wait_ge(p_ready, n7 + (l + 1))
                        pe.wait_ge(tt_ready, n7 + l)
                        if l == 1:
                            pe.wait_ge(attn_ready, n1)
                        for t in range(NT):
                            ins = pe.matmul(bch(7)[:, t, :], p_sb[l % 2][:, t, :], tt_sb[(l - 1) % 2][:, t, :], start=True, stop=True)
                        ins.then_inc(tt_done, 1)

                    def logits(g):
                        if g:
                            pe.wait_ge(pv_read[0], n1)
                        else:
                            pe.wait_ge(kd_ready, n1)
                        for t in range(NT):
                            cc = g * NT + t
                            ins = pe.matmul(bch(3)[:, t, :], qbd[:, par, cc, :], kb[:, cc * CH:cc * CH + P], start=True, stop=True)
                        ins.then_inc(lg_done[g], 1)

                    def probs(g):
                        pe.wait_ge(prob_ready[g], n1)
                        pe.wait_ge(vr_ready if g == 0 else pts_ready[0], n1)
                        for t in range(NT):
                            ins = pe.transpose(bch(4)[:, t, :], lg[:, t, :], ident)
                        ins.then_inc(prt_done[g], 1)

                    def values(g):
                        pe.wait_ge(vwin_ready, b1 * 2)
                        pe.wait_ge(pts_ready[g], n1)
                        for t in range(NT):
                            ins = pe.matmul(bch(3)[:, t, :], vwin[:, g * NT + t, :], pts[:, t, :], start=True, stop=True)
                        ins.then_inc(pv_done[g], 1)

                    pe.wait_ge(dec_ready, n1)
                    pe.wait_ge(pt_ready, n6 + 1)
                    for t in range(NT):
                        ins = pe.transpose(bch(5)[:, t, :], pt_sb[0][:, t, :], ident)
                    ins.then_inc(p_done, 1)
                    fill(2)
                    square(1)
                    fill(1)
                    square(2)
                    accumulate(1)
                    logits(0)
                    fill(1)
                    square(3)
                    accumulate(2)
                    fill(1)
                    square(4)
                    accumulate(3)
                    fill(1)
                    square(5)
                    accumulate(4)
                    probs(0)
                    fill(1)
                    square(6)
                    accumulate(5)
                    values(0)
                    fill(1)
                    accumulate(6)
                    logits(1)
                    fill(1)
                    tt = tt_sb[LEVELS % 2]
                    pe.wait_ge(tt_ready, n7 + (LEVELS + 1))
                    for t in range(NT):
                        c = slice(t * P, (t + 1) * P)
                        pe.wait_ge(s_ready if t else s0_ready, n4 + t if t else n1)
                        pe.matmul(bank[5][:, 0:P], k[:, c], s_cur[:, t % 2, :], start=True, stop=True).then_inc(ks_done, 1)
                        if t:
                            pe.wait_ge(o1_ready, n4 + t)
                        else:
                            pe.wait_ge(ssq_ready[0], n1)
                        pe.matmul(bank[2][:, 0:P], q[:, c], s_cur[:, t % 2, :], start=True, stop=True).then_inc(qs_done, 1)
                        fill(2 if t else 3)
                        pe.wait_ge(r_ready, n4 + (t + 1))
                        pe.matmul(bank[5][:, 0:P], tt[:, t, :], r_sb[:, :], start=True, stop=True).then_inc(y_done, 1)
                        if t == 1:
                            probs(1)
                        fill(1)
                        pe.wait_ge(y_ready, n4 + (t + 1))
                        pe.matmul(bank[6][:, 0:P], kd[:, t, :], y_sb[:, t % 2, :], start=True, stop=True).then_inc(ds_done, 1)
                        if t:
                            pe.wait_ge(o_ready, n4 + t)
                        pe.matmul(bank[7][:, 0:P], attn[:, t, :], y_sb[:, t % 2, :], start=True, stop=True).then_inc(ay_done, 1)
                        if t == 1:
                            values(1)
                        fill(1)
                    fill(99)
                    pe.wait_ge(o1_ready, n4 + NT)
                    pe.wait_ge(pv_read[1], n1)
                    pe.wait_ge(pts_ready[1], n1)
                    pe.wait_ge(on_ready, n1)
                    for t in range(NT):
                        ins = pe.transpose(bch(4)[:, t, :], o_sb[:, t, :], ident)
                    ins.then_inc(ot_done, 1)

                def prepare(hh):
                    uu = pe.snap(b * PAIRS + hh * (HEAD_TILES // 2) + (PRO_TILES // 2 + 1))
                    vv = pe.snap(b * EVACS + hh * (HEAD_TILES // 2) + (PRO_TILES // 2 + 1))
                    return project(uu, vv)

                def pair(first, h0, last):
                    for par in range(2):
                        n1 = pe.snap(first + (par + 1))
                        gen = iter(()) if last and par else prepare(h0 + (par + 1))

                        def fill(n):
                            for _ in range(n):
                                next(gen, None)
                        head(par, n1, fill)

                for i, _ in enumerate(prepare(0)):
                    if i == 2 * KT - 2:
                        sum_decays()
                with pe.Fori(0, H // 2 - 1) as hp:
                    pair(b * H + hp * 2, hp * 2, False)
                pair(b * H + (H - 2), H - 2, True)

                with pe.Fori(0, KT) as c:
                    uu = pe.snap(b * PAIRS + c * 2 + ((PRO_TILES + H * HEAD_TILES) // 2 + 1))
                    vv = pe.snap(b * EVACS + c * 2 + ((PRO_TILES + H * HEAD_TILES) // 2 + 1))
                    gemm(0, uu, vv, hT_hi, hT_lo)
                    pe.wait_ge(head_dve_done, b1 * H + 2)
                    gemm(1, uu, vv, oa_hi, oa_lo)
                    gemm(0, uu + 1, vv + 1, hT_hi, hT_lo)
                    gemm(1, uu + 1, vv + 1, ob_hi, ob_lo)

                for s in range(2):
                    pe.wait_ge(z_read[s], b1 * EVACS + 1)
                for n in range(2):
                    for q in range(NT):
                        s = q % 2
                        un = u + (PAIRS - OUT_TILES // 2 + n * 2 + q // 2)
                        pe.wait_ge(hi_ready[s], un)
                        pe.wait_ge(lo_ready[s], un)
                        if n and q == 0:
                            pe.wait_ge(res_half, b1)
                        if n == 0:
                            for k in (2 * q, 2 * q + 1):
                                pe.wait_ge(m_hi[k], b1)
                                pe.wait_ge(m_lo[k], b1)
                        for t in range(NT):
                            for kk in range(2):
                                k = 2 * q + kk
                                c = slice(t * P, (t + 1) * P)
                                wc = slice(kk * TB, (kk + 1) * TB)
                                ins = split_mm(bank[OUT_BANKS[n][t]][:, :], oa_hi[:, k, c], oa_lo[:, k, c],
                                               w_hi[:, s, wc], w_lo[:, s, wc], k == 0, k == KT - 1)
                        ins.then_inc(gemm_done[s], 1)
                        if n:
                            if q == 0:
                                pe.wait_ge(x_normed, b1 + 1)
                            transpose_x(b1, 2 * q)
                            transpose_x(b1, 2 * q + 1)


OUT_BANKS = ((2, 3, 4, 5), (6, 7, 2, 3))


def relative_buckets():
    nb, dist = 16, 128
    rel = np.arange(2 * CH)[None, :] - CH - np.arange(CH)[:, None]
    n = np.abs(rel)
    exact = nb // 2
    large = exact + (np.log(np.maximum(n, 1) / exact) / np.log(dist / exact) * (nb - exact)).astype(np.int32)
    return ((rel > 0) * nb + np.where(n < exact, n, np.minimum(large, nb - 1))).astype(np.int32)


def kernel(x, norm_w, w_in, conv_w, a_log, dt_bias, gdn_norm_w, attn_sinks, w_o_a, w_o_b, w_out, rel_bias, final_norm_w):
    import concourse.bacc as bacc
    from concourse.bass_utils import run_bass_kernel_spmd

    x, norm_w, w_in, conv_w, a_log, dt_bias, gdn_norm_w, attn_sinks, w_o_a, w_o_b, w_out, rel_bias, final_norm_w = (
        np.asarray(a) for a in (x, norm_w, w_in, conv_w, a_log, dt_bias, gdn_norm_w, attn_sinks, w_o_a, w_o_b, w_out,
                                rel_bias, final_norm_w))
    f32 = np.float32
    w = w_in[0]
    at = np.cumsum([0, D, D, D, H, H, D, D, 2 * DH, 2 * DH, D, D, D])
    (qa, ka, va, b_a, a_a, z_a, qb, kb_, vb_, z_b, g_a, g_b) = (w[:, at[i]:at[i + 1]] for i in range(12))

    def tile(m):
        return m.reshape(KT, P, P).transpose(1, 0, 2).reshape(P, TILE)

    def head(m, h):
        return m[:, h * P:(h + 1) * P]

    pair = np.arange(D).reshape(2, H, DH).transpose(1, 0, 2).reshape(-1)
    qb, z_b, wob = qb[:, pair], z_b[:, pair], w_o_b[0][pair]
    ba_w = np.concatenate([b_a, a_a, np.zeros((D, P - 2 * H), f32)], axis=1)
    tiles = [tile(kb_), tile(vb_), tile(ba_w), np.zeros((P, TILE), f32)]
    for h in range(H):
        tiles += [tile(head(m, h)) for m in (qa, ka, va, qb, z_a, z_b)]
    for c in range(KT):
        tiles += [tile(head(m, c)) for m in (g_a, w_o_a[0], g_b, wob)]
    for n in range(2):
        for q in range(NT):
            m = w_out[0][2 * q * P:(2 * q + 2) * P, n * TB:(n + 1) * TB]
            tiles.append(m.reshape(2, P, TB).transpose(1, 0, 2).reshape(P, TILE))
    w_tiles = np.stack(tiles + tiles[:2])

    conv = conv_w[0].reshape(CONV, 3, H, P).transpose(2, 3, 1, 0).reshape(H, P, 3 * CONV)
    sinks = np.repeat(attn_sinks[0].reshape(2, H).T, CH, axis=1)[:, :, None]
    step_const = np.concatenate([conv, sinks], axis=2)
    full = rel_bias[relative_buckets()].transpose(2, 0, 1)
    full = full.reshape(2, H, CH, P).transpose(1, 0, 2, 3).reshape(H, P, P)
    bias = np.empty((NB, H, P, 2, P), f32)
    bias[:, :, :, 0] = full
    bias[:, :, :, 1] = full
    bias[0, :, :, 0, 0:CH] = NEG
    bias = bias.reshape(NB * H, P, 2, P)

    i = np.arange(P)
    masks = np.stack([np.eye(P), i[:, None] <= i[None, :], i[:, None] > i[None, :], -1.0 * (i[:, None] < i[None, :]),
                      np.ones((P, P))]).astype(f32).transpose(1, 0, 2)
    xb = x[0].reshape(NB, NT, P, D).transpose(0, 2, 1, 3)
    ins = {
        "x": np.concatenate([xb, xb[:1]]),
        "w_tiles": w_tiles,
        "norm_w": norm_w[0].reshape(KT, P).T,
        "gdn_norm_w": gdn_norm_w[0][:, None],
        "decay_bias": np.broadcast_to(np.stack([a_log[0], dt_bias[0]])[None], (P, 2, H)),
        "step_const": step_const,
        "bias": bias,
        "final_w": np.broadcast_to(final_norm_w[None], (P, D)),
        "masks": masks,
    }
    nc = bacc.Bacc("TRN2", target_bir_lowering=False, num_devices=1, dynamic_dma_scratch_size=1024)
    arrays, args = {}, []
    for name, a in ins.items():
        a = np.ascontiguousarray(a)
        arrays[f"in_{name}"] = a
        args.append(nc.dram_tensor(f"in_{name}", a.shape, mybir.dt.from_np(a.dtype), kind="ExternalInput").ap())
    out = nc.dram_tensor("out_y", (NB, P, NT, D), F32, kind="ExternalOutput").ap()
    build_program(nc, *args, out)
    res = run_bass_kernel_spmd(nc, [arrays], core_ids=[0])
    y = res.results[0]["out_y"]
    return np.ascontiguousarray(y.transpose(0, 2, 1, 3)).reshape(1, SEQ, D)
```
